# Optimizing a Trainium2 kernel written in Bass

```python
import jax, jax.numpy as jnp
from jax import lax
import numpy as np

D_MODEL = 1024
BATCH = 1
SEQ = 512
DEPTH = 2

D_CONV = D_MODEL
CONV_WIDTH = 3
SGU_HEADS = 8
SGU_HEAD_DIM = 128
SGU_CHUNK = 128
D_SGU = SGU_HEADS * SGU_HEAD_DIM
ATTN_HEADS = 8
ATTN_HEAD_DIM = 128
D_ATTN = ATTN_HEADS * ATTN_HEAD_DIM
Q_BLOCK = 128
N_BRANCH = 3
D_FF = 2816
RMS_EPS = 1e-6
LN_EPS = 1e-5
FORGET_W_SCALE = 0.1
FORGET_BIAS = 3.0
SPLIT_SIZES = (D_CONV, D_CONV, D_CONV, D_SGU, D_SGU, D_ATTN, D_ATTN, D_ATTN, ATTN_HEADS, N_BRANCH * D_MODEL)
N_IN = 3 * D_CONV + 2 * D_SGU + 3 * D_ATTN + ATTN_HEADS + N_BRANCH * D_MODEL
FORGET_OFFSET = 3 * D_CONV + 2 * D_SGU + 3 * D_ATTN

kernel_name = "hybrid_conv_sgu_fox_macaron"

def rms_norm(x, g):
    xf = x.astype(jnp.float32)
    y = xf * lax.rsqrt(jnp.mean(xf * xf, axis=-1, keepdims=True) + RMS_EPS)
    return (y * g.astype(jnp.float32)).astype(x.dtype)

def layer_norm(x, g, b):
    xf = x.astype(jnp.float32)
    mu = jnp.mean(xf, axis=-1, keepdims=True)
    var = jnp.mean(jnp.square(xf - mu), axis=-1, keepdims=True)
    y = (xf - mu) * lax.rsqrt(var + LN_EPS)
    return (y * g.astype(jnp.float32) + b.astype(jnp.float32)).astype(x.dtype)

def swiglu(x, w_gu, w_down):
    g, u = jnp.split(x @ w_gu, 2, axis=-1)
    return (jax.nn.silu(g) * u) @ w_down

def causal_depthwise_conv(z, w):
    K = w.shape[0]
    zp = jnp.pad(z, ((0, 0), (K - 1, 0), (0, 0)))
    return lax.conv_general_dilated(
        zp, w[:, None, :], window_strides=(1,), padding='VALID',
        dimension_numbers=('NWC', 'WIO', 'NWC'), feature_group_count=z.shape[-1])

def chunked_spatial_gating(u, v, ln_g, ln_b, w_s, b_s):
    bsz, s_len, _ = v.shape
    n_chunks = s_len // SGU_CHUNK
    vn = layer_norm(v, ln_g, ln_b).reshape(bsz, n_chunks, SGU_CHUNK, SGU_HEADS, SGU_HEAD_DIM)
    causal = jnp.tril(jnp.ones((SGU_CHUNK, SGU_CHUNK), dtype=bool))
    w = jnp.where(causal[None], w_s, jnp.zeros((), w_s.dtype))
    s = jnp.einsum('gts,bnsgc->bntgc', w, vn) + b_s.T[None, None, :, :, None]
    return u * s.reshape(bsz, s_len, D_SGU)

def forgetting_attention(q, k, v, log_f):
    c = jnp.cumsum(log_f, axis=1).transpose(0, 2, 1)
    scale = ATTN_HEAD_DIM ** -0.5
    s_len = q.shape[1]
    outs = []
    for i in range(s_len // Q_BLOCK):
        q0 = i * Q_BLOCK
        q1 = q0 + Q_BLOCK
        logits = jnp.einsum('bqhd,bkhd->bhqk', q[:, q0:q1], k[:, :q1]).astype(jnp.float32) * scale
        decay = c[:, :, q0:q1, None] - c[:, :, None, :q1]
        causal = jnp.arange(q1)[None, :] <= jnp.arange(q0, q1)[:, None]
        logits = jnp.where(causal, logits + decay, -jnp.inf)
        p = jax.nn.softmax(logits, axis=-1)
        outs.append(jnp.einsum('bhqk,bkhd->bqhd', p.astype(v.dtype), v[:, :q1]))
    return jnp.concatenate(outs, axis=1)

def setup_inputs(seed: int = 0) -> dict:
    key = jax.random.key(seed)
    ks = jax.random.split(key, 24)
    L, D = DEPTH, D_MODEL

    def dense(k, shape, fan_in):
        return jax.random.normal(k, shape, jnp.float32) * (fan_in ** -0.5)

    def gain(k, shape):
        return 1.0 + 0.02 * jax.random.normal(k, shape, jnp.float32)

    w_in = dense(ks[5], (L, D, N_IN), D)
    w_in = w_in.at[:, :, FORGET_OFFSET:FORGET_OFFSET + ATTN_HEADS].multiply(FORGET_W_SCALE)
    return {
        "x": jax.random.normal(ks[0], (BATCH, SEQ, D), jnp.float32),
        "ffn1_norm": gain(ks[1], (L, D)),
        "ffn1_w_gu": dense(ks[2], (L, D, 2 * D_FF), D),
        "ffn1_w_down": dense(ks[3], (L, D_FF, D), D_FF),
        "mix_norm": gain(ks[4], (L, D)),
        "w_in": w_in,
        "b_forget": FORGET_BIAS + 0.5 * jax.random.normal(ks[6], (L, ATTN_HEADS), jnp.float32),
        "b_gate": 0.02 * jax.random.normal(ks[7], (L, N_BRANCH, D), jnp.float32),
        "conv_w": dense(ks[8], (L, CONV_WIDTH, D_CONV), CONV_WIDTH),
        "sgu_ln_g": gain(ks[9], (L, D_SGU)),
        "sgu_ln_b": 0.02 * jax.random.normal(ks[10], (L, D_SGU), jnp.float32),
        "sgu_w": dense(ks[11], (L, SGU_HEADS, SGU_CHUNK, SGU_CHUNK), SGU_CHUNK),
        "sgu_b": gain(ks[12], (L, SGU_HEADS, SGU_CHUNK)),
        "q_norm_g": gain(ks[13], (L, ATTN_HEADS, ATTN_HEAD_DIM)),
        "k_norm_g": gain(ks[14], (L, ATTN_HEADS, ATTN_HEAD_DIM)),
        "w_out_conv": dense(ks[15], (L, D_CONV, D), D_CONV),
        "w_out_sgu": dense(ks[16], (L, D_SGU, D), D_SGU),
        "w_out_attn": dense(ks[17], (L, D_ATTN, D), D_ATTN),
        "w_o": dense(ks[18], (L, D, D), D),
        "ffn2_norm": gain(ks[19], (L, D)),
        "ffn2_w_gu": dense(ks[20], (L, D, 2 * D_FF), D),
        "ffn2_w_down": dense(ks[21], (L, D_FF, D), D_FF),
    }

def reference(x, ffn1_norm, ffn1_w_gu, ffn1_w_down, mix_norm, w_in, b_forget, b_gate, conv_w,
              sgu_ln_g, sgu_ln_b, sgu_w, sgu_b, q_norm_g, k_norm_g, w_out_conv, w_out_sgu,
              w_out_attn, w_o, ffn2_norm, ffn2_w_gu, ffn2_w_down):
    bsz, s_len, _ = x.shape
    split_idx = []
    acc = 0
    for sz in SPLIT_SIZES[:-1]:
        acc += sz
        split_idx.append(acc)

    for l in range(DEPTH):
        x = x + 0.5 * swiglu(rms_norm(x, ffn1_norm[l]), ffn1_w_gu[l], ffn1_w_down[l])

        h = rms_norm(x, mix_norm[l])
        a_b, a_c, a_x, s_u, s_v, q, k, v, f_logit, g_logit = jnp.split(h @ w_in[l], split_idx, axis=-1)

        y_a = (a_b * causal_depthwise_conv(a_c * a_x, conv_w[l])) @ w_out_conv[l]

        u = jax.nn.gelu(s_u, approximate=False)
        vv = jax.nn.gelu(s_v, approximate=False)
        y_b = chunked_spatial_gating(u, vv, sgu_ln_g[l], sgu_ln_b[l], sgu_w[l], sgu_b[l]) @ w_out_sgu[l]

        q = rms_norm(q.reshape(bsz, s_len, ATTN_HEADS, ATTN_HEAD_DIM), q_norm_g[l])
        k = rms_norm(k.reshape(bsz, s_len, ATTN_HEADS, ATTN_HEAD_DIM), k_norm_g[l])
        v = v.reshape(bsz, s_len, ATTN_HEADS, ATTN_HEAD_DIM)
        log_f = jax.nn.log_sigmoid(f_logit.astype(jnp.float32) + b_forget[l].astype(jnp.float32))
        y_c = forgetting_attention(q, k, v, log_f).reshape(bsz, s_len, D_ATTN) @ w_out_attn[l]

        gates = jax.nn.sigmoid(g_logit.reshape(bsz, s_len, N_BRANCH, D_MODEL) + b_gate[l])
        merged = gates[:, :, 0] * y_a + gates[:, :, 1] * y_b + gates[:, :, 2] * y_c
        x = x + merged @ w_o[l]

        x = x + 0.5 * swiglu(rms_norm(x, ffn2_norm[l]), ffn2_w_gu[l], ffn2_w_down[l])
    return x


_drawn_inputs = setup_inputs


def setup_inputs(seed=0):
    import zlib

    import numpy as np

    out = dict(_drawn_inputs(seed))
    spreads = {}
    factors = {'ffn1_norm': 3.735,
     'b_gate': 8.0,
     'sgu_ln_g': 35.491,
     'sgu_ln_b': 37.489,
     'sgu_b': 25.749,
     'q_norm_g': 48.425,
     'k_norm_g': 47.829,
     'ffn2_norm': 5.878,
     'b_forget': 21.64}
    for name, (base, spread) in spreads.items():
        noise = np.random.default_rng([zlib.crc32(name.encode()), seed]).standard_normal(out[name].shape)
        drawn = base * np.exp(spread * noise) if base else spread * noise
        out[name] = __import__('jax').numpy.asarray(drawn.astype(out[name].dtype))
    for name, factor in factors.items():
        out[name] = (out[name] * factor).astype(out[name].dtype)
    return out
```

```python
from contextlib import ExitStack

import concourse.bass as bass
from concourse import mybir

ALU = mybir.AluOpType
ACT = mybir.ActivationFunctionType
AX_X = mybir.AxisListType.X
F32 = mybir.dt.float32
F32R = mybir.dt.float32r
BF16 = mybir.dt.bfloat16

P = 128
RMS_EPS = 1e-6
LN_EPS = 1e-5
MASKED = -1e30


def ds(start, n):
    return bass.ds(start, n)


def build(nc, x, ffn1_norm, ffn1_w_gu, ffn1_w_down, mix_norm, w_in, b_forget, b_gate, conv_w,
          sgu_ln_g, sgu_ln_b, sgu_w, sgu_b, q_norm_g, k_norm_g, w_out_conv, w_out_sgu,
          w_out_attn, w_o, ffn2_norm, ffn2_w_gu, ffn2_w_down, out):
    L, D, _ = ffn1_w_gu.shape
    S = x.shape[1]
    FF = ffn1_w_down.shape[1]
    H = b_forget.shape[1]
    KB = D // P
    FB = FF // P
    TB = S // P
    W = 2 * P
    NJ = D // W
    NU = FF // W
    HK = FB // 2
    CELLS = KB * W
    SC = float(P) ** -0.5
    assert H == KB and x.shape[0] == 1 and NJ == 4 and FB % 2 == 0 and HK * P <= CELLS and TB == 4

    C_B, C_C, C_X, C_SU, C_SV, C_Q, C_K, C_V = (n * D for n in range(8))
    C_F = 8 * D
    C_G = C_F + H

    T_UP1, T_DN1, T_A, T_WA, T_BV, T_BU, T_WB, T_C, T_WC, T_WO, T_UP2, T_DN2, T_ALL = (
        0, NU, NU + KB, NU + KB + 8, NU + KB + 10, NU + KB + 12, NU + KB + 16, NU + KB + 18,
        NU + KB + 26, NU + KB + 28, NU + KB + 30, 2 * NU + KB + 30, 2 * NU + 2 * KB + 30)
    U_UP1, U_DN1, U_A, U_WA, U_BV, U_BU, U_WB, U_C, U_WC, U_WO, U_UP2, U_DN2, U_ALL = (
        0, NU, NU + NJ, NU + NJ + 8, NU + NJ + 10, NU + NJ + 12, NU + NJ + 16, NU + NJ + 18,
        NU + NJ + 30, NU + NJ + 32, NU + NJ + 34, 2 * NU + NJ + 34, 2 * NU + 2 * NJ + 34)

    CONSTS = 6

    R_MIX, R_CONV, R_GATE, R_Q, R_K, R_FFN2, R_NEXT = 0, KB, 4 * KB, 7 * KB, 8 * KB, 9 * KB, 10 * KB
    ROWS = 11 * KB

    Q_OFF = [896, 1024, 512, 0]
    K_OFF = [0, 512, 1024, 896]
    PACKED = 1280

    with ExitStack() as ctx:
        def sem(name):
            return ctx.enter_context(nc.semaphore(name))

        def sb(name, shape, dt=F32, stack=ctx):
            return stack.enter_context(nc.sbuf_tensor(name, shape, dt))

        ps = ctx.enter_context(nc.psum_tensor("ps", [P, 8, S], F32))
        ps_flat = ps[:].rearrange("p b s -> p (b s)")
        packed = ps_flat[:, 4 * S:4 * S + PACKED]

        xT = sb("xT", [P, KB, S])
        h_hi = sb("h_hi", [P, KB, S], F32R)
        h_lo = sb("h_lo", [P, KB, S], F32R)
        raw = sb("raw", [P, 2, CELLS])
        w_hi = sb("w_hi", [P, 2, CELLS], F32R)
        w_lo = sb("w_lo", [P, 2, CELLS], F32R)
        rinv = sb("rinv", [P, S])
        rtok = sb("rtok", [P, TB])
        t_a = sb("t_a", [P, 2, S])
        t_b = sb("t_b", [P, 2, S])
        sq = sb("sq", [P, 2, S])
        y_c = sq
        cn_bc = sq
        ident = sb("ident", [P, P])
        ident_b = sb("ident_b", [P, P], BF16)
        causal_b = sb("causal_b", [P, P], BF16)
        upper = sb("upper", [P, P])
        lower = sb("lower", [P, P])
        ones = sb("ones", [P, P])
        rows = sb("rows", [P, P])
        par = sb("par", [P, ROWS])
        wf_raw = sb("wf_raw", [P, KB, H])
        wf_hi = sb("wf_hi", [P, KB, H], F32R)
        wf_lo = sb("wf_lo", [P, KB, H], F32R)
        bf_bc = sb("bf_bc", [P, H])
        c_tok = sb("c_tok", [P, TB, H])
        nmax = sb("nmax", [P, 2, TB])
        esum = sb("esum", [P, 2, TB])
        stats = sb("stats", [P, TB, 2, 6])
        mv = sb("mv", [P, TB, 2])
        rstd = sb("rstd", [P, TB])
        eps_rms = sb("eps_rms", [P, 1])
        eps_ln = sb("eps_ln", [P, 1])
        c_dram = nc.dram_tensor("c_scratch", (H, S), F32, kind="Internal").ap()

        with ExitStack() as ffn:
            act_hi = sb("act_hi", [P, FB, S], F32R, ffn)
            act_lo = sb("act_lo", [P, FB, S], F32R, ffn)
        with ExitStack() as ends:
            x_io = sb("x_io", [P, TB, D], F32, ends)
        br_hi = sb("br_hi", [P, KB, S], F32R)
        br_lo = sb("br_lo", [P, KB, S], F32R)
        gate = sb("gate", [P, KB, S])
        merged = sb("merged", [P, KB, S])
        with ExitStack() as b_mem:
            sw_raw = sb("sw_raw", [P, H, P], F32, b_mem)
            bs_bc = sb("bs_bc", [P, H, P], F32, b_mem)
            with ExitStack() as a_mem:
                z = sb("z", [P, 2, S + 2], F32, a_mem)
                c_neg = sb("c_neg", [H, S], F32, a_mem)
                lf = sb("lf", [P, 6, TB, H], F32, a_mem)
            vn = sb("vn", [P, TB, D], F32, b_mem)
            vn_hi = sb("vn_hi", [P, TB, W], F32R, b_mem)
            vn_lo = sb("vn_lo", [P, TB, W], F32R, b_mem)
            sw_hi = sb("sw_hi", [P, H, P], F32R, b_mem)
            sw_lo = sb("sw_lo", [P, H, P], F32R, b_mem)
        with ExitStack() as c_mem:
            q_hi = sb("q_hi", [P, 2, S], F32R, c_mem)
            q_lo = sb("q_lo", [P, 2, S], F32R, c_mem)
            k_hi = sb("k_hi", [P, 2, S], F32R, c_mem)
            k_lo = sb("k_lo", [P, 2, S], F32R, c_mem)
            v_hi = sb("v_hi", [P, TB, W], F32R, c_mem)
            v_lo = sb("v_lo", [P, TB, W], F32R, c_mem)
            prob = sb("prob", [P, 2, PACKED], F32, c_mem)
            pt_hi = sb("pt_hi", [P, PACKED], F32R, c_mem)
            pt_lo = sb("pt_lo", [P, PACKED], F32R, c_mem)
        m_hi = sb("m_hi", [P, KB, S], F32R)
        m_lo = sb("m_lo", [P, KB, S], F32R)
        ln_g = gate[:, 0:2, :].rearrange("p a s -> p (a s)")
        ln_b = gate[:, 2:4, :].rearrange("p a s -> p (a s)")

        raw_in = [sem("raw_in0"), sem("raw_in1")]
        hi_rdy = [sem("hi_rdy0"), sem("hi_rdy1")]
        lo_rdy = [sem("lo_rdy0"), sem("lo_rdy1")]
        tile_done = [sem("tile_done0"), sem("tile_done1")]
        drained = [sem("drained0"), sem("drained1")]
        rows_in, wf_in, bf_in, x_in = sem("rows_in"), sem("wf_in"), sem("bf_in"), sem("x_in")
        sw_in, bs_in, lng_in, lnb_in, cn_in = sem("sw_in"), sem("bs_in"), sem("lng_in"), sem("lnb_in"), sem("cn_in")
        c_out, y_out = sem("c_out"), sem("y_out")
        const_rdy = sem("const_rdy")
        par_mm, par_rdy = sem("par_mm"), sem("par_rdy")
        x_mm, x_copied = sem("x_mm"), sem("x_copied")
        h_hi_rdy, h_rdy = sem("h_hi_rdy"), sem("h_rdy")
        sq_rdy, ssq_rdy = sem("sq_rdy"), sem("ssq_rdy")
        rms_mm, rms_sqrt, rms_rdy = sem("rms_mm"), sem("rms_sqrt"), sem("rms_rdy")
        silu_rdy, up_prod, act_hi_rdy, act_rdy = sem("silu_rdy"), sem("up_prod"), sem("act_hi_rdy"), sem("act_rdy")
        wf_hi_rdy, wf_rdy, f_mm, f_steps, f_exp, f_ln, f_rdy = (
            sem("wf_hi_rdy"), sem("wf_rdy"), sem("f_mm"), sem("f_steps"), sem("f_exp"), sem("f_ln"), sem("f_rdy"))
        f_chain = sem("f_chain")
        c_mm, c_copied = sem("c_mm"), sem("c_copied")
        z_pad, z_rdy, conv0, conv1, conv2 = sem("z_pad"), sem("z_rdy"), sem("conv0"), sem("conv1"), sem("conv2")
        br_prod, br_hi_rdy, br_rdy = sem("br_prod"), sem("br_hi_rdy"), sem("br_rdy")
        gate_rdy = sem("gate_rdy")
        mg_add, m_hi_rdy, m_rdy = sem("mg_add"), sem("m_hi_rdy"), sem("m_rdy")
        sw_masked, sw_mm, sw_hi_rdy, sw_rdy = sem("sw_masked"), sem("sw_mm"), sem("sw_hi_rdy"), sem("sw_rdy")
        ln_stats, ln_mv, ln_sqrt, ln_rstd, ln_norm = (
            sem("ln_stats"), sem("ln_mv"), sem("ln_sqrt"), sem("ln_rstd"), sem("ln_norm"))
        ln_gained, vn_rdy = sem("ln_gained"), sem("vn_rdy")
        gelu_rdy, vn_hi_rdy, vns_rdy, sp_mm, sp_added = (
            sem("gelu_rdy"), sem("vn_hi_rdy"), sem("vns_rdy"), sem("sp_mm"), sem("sp_added"))
        qk_sq, qk_mm, qk_inv, qk_norm = sem("qk_sq"), sem("qk_mm"), sem("qk_inv"), sem("qk_norm")
        q_hi_rdy, q_rdy, k_hi_rdy, k_rdy = sem("q_hi_rdy"), sem("q_rdy"), sem("k_hi_rdy"), sem("k_rdy")
        v_hi_rdy = sem("v_hi_rdy")
        s_mm, s_taken, s_max, s_exp, s_rcp, p_rdy = (
            sem("s_mm"), sem("s_taken"), sem("s_max"), sem("s_exp"), sem("s_rcp"), sem("p_rdy"))
        pt_mm, pt_hi_rdy, pt_rdy, pv_mm, pv_hi_rdy, pv_taken = (
            sem("pt_mm"), sem("pt_hi_rdy"), sem("pt_rdy"), sem("pv_mm"), sem("pv_hi_rdy"), sem("pv_taken"))
        y_mm, y_copied = sem("y_mm"), sem("y_copied")

        block = ctx.enter_context(nc.Block())

        def over_pair(ap):
            return ap.unsqueeze(1).broadcast_to([P, 2, S])

        def pair(p):
            return ps[:, 2 * p:2 * p + 2, :]

        @block.sync
        def _(sp):
            def load(dst, src, done):
                sp.dma_start(dst, src).then_inc(done, 16)

            def wide(s, T, w, l, c0):
                sp.wait_ge(lo_rdy[s], T)
                load(raw[:, s, :].rearrange("p (k n) -> p k n", n=W),
                     w[ds(l, 1), :, ds(c0, W)].rearrange("l (k p) n -> p (l k) n", p=P), raw_in[s])

            def tall(s, T, w, l, d):
                sp.wait_ge(lo_rdy[s], T)
                load(raw[:, s, 0:HK * P].rearrange("p (k n) -> p k n", n=P),
                     w[ds(l, 1), s * HK * P:(s + 1) * HK * P, ds(d * P, P)].rearrange(
                         "l (k p) n -> p (l k) n", p=P), raw_in[s])

            def param_rows(r, vec, l):
                v = vec[ds(l, 1)]
                v = v.rearrange("l (j p) -> (l j) p", p=P) if len(vec.shape) == 2 else \
                    v.rearrange("l w (j p) -> (l w j) p", p=P) if vec.shape[-1] > P else \
                    v.rearrange("l h p -> (l h) p")
                load(rows[r:r + v.shape[0], :], v, rows_in)

            load(x_io[:], x[0].rearrange("(t p) d -> p t d", p=P), x_in)
            param_rows(0, ffn1_norm, 0)

            def ffn(l, w_gu, w_down, t_up, t_dn):
                with sp.Fori(0, NU) as i:
                    wide(0, l * T_ALL + t_up + i, w_gu, l, i * W)
                    wide(1, l * T_ALL + t_up + i, w_gu, l, FF + i * W)
                with sp.Fori(0, KB) as d:
                    tall(0, l * T_ALL + t_dn + d, w_down, l, d)
                    tall(1, l * T_ALL + t_dn + d, w_down, l, d)

            def square_matrix(l, w, t0):
                with sp.Fori(0, 2) as i:
                    for s in range(2):
                        wide(s, l * T_ALL + t0 + i, w, l, (2 * i + s) * W)

            with sp.Fori(0, L) as l:
                sp.wait_ge(par_mm, l + 1)
                param_rows(R_MIX, mix_norm, l)
                param_rows(R_CONV, conv_w, l)
                param_rows(R_GATE, b_gate, l)
                param_rows(R_Q, q_norm_g, l)
                param_rows(R_K, k_norm_g, l)
                param_rows(R_FFN2, ffn2_norm, l)
                param_rows(R_NEXT, ffn1_norm, (l + 1) % L)
                sp.wait_ge(wf_rdy, l)
                load(wf_raw[:], w_in[ds(l, 1), :, C_F:C_F + H].rearrange("l (k p) n -> p (l k) n", p=P), wf_in)
                sp.wait_ge(f_steps, 2 * l)
                load(bf_bc[:], b_forget[ds(l, 1)].rearrange("l h -> (l h)").partition_broadcast(P), bf_in)

                ffn(l, ffn1_w_gu, ffn1_w_down, T_UP1, T_DN1)
                with sp.Fori(0, NJ) as i:
                    T = l * T_ALL + T_A + 2 * i
                    wide(0, T, w_in, l, C_C + i * W)
                    wide(1, T, w_in, l, C_X + i * W)
                    wide(0, T + 1, w_in, l, C_B + i * W)
                    wide(1, T + 1, w_in, l, C_G + i * W)
                sp.wait_ge(tile_done[1], l * T_ALL + T_A)
                load(sw_raw[:], sgu_w[ds(l, 1)].rearrange("l g t s -> t (l g) s"), sw_in)
                load(bs_bc[:], sgu_b[ds(l, 1)].rearrange("l g t -> (l g) t").partition_broadcast(P), bs_in)
                square_matrix(l, w_out_conv, T_WA)
                sp.wait_ge(c_copied, 2 * l + 2)
                sp.dma_start(c_dram, c_neg[:]).then_inc(c_out, 16)
                with sp.Fori(0, 2) as i:
                    for s in range(2):
                        wide(s, l * T_ALL + T_BV + i, w_in, l, C_SV + (2 * i + s) * W)
                sp.wait_ge(c_out, 16 * (l + 1))
                load(ln_g, sgu_ln_g[ds(l, 1)].rearrange("l d -> (l d)").partition_broadcast(P), lng_in)
                load(ln_b, sgu_ln_b[ds(l, 1)].rearrange("l d -> (l d)").partition_broadcast(P), lnb_in)
                with sp.Fori(0, NJ) as i:
                    wide(0, l * T_ALL + T_BU + i, w_in, l, C_SU + i * W)
                    wide(1, l * T_ALL + T_BU + i, w_in, l, C_G + D + i * W)
                square_matrix(l, w_out_sgu, T_WB)
                with sp.Fori(0, NJ) as i:
                    T = l * T_ALL + T_C + 2 * i
                    wide(0, T, w_in, l, C_Q + i * W)
                    wide(1, T, w_in, l, C_K + i * W)
                    wide(0, T + 1, w_in, l, C_V + i * W)
                    sp.wait_ge(s_taken, l * H + 2 * i)
                    load(cn_bc[:], c_dram[ds(2 * i, 2), :].partition_broadcast(P), cn_in)
                    wide(1, T + 1, w_in, l, C_G + 2 * D + i * W)
                square_matrix(l, w_out_attn, T_WC)
                square_matrix(l, w_o, T_WO)
                ffn(l, ffn2_w_gu, ffn2_w_down, T_UP2, T_DN2)
            wide(0, L * T_ALL, ffn1_w_gu, 0, 0)
            wide(1, L * T_ALL, ffn1_w_gu, 0, FF)
            for t in range(TB):
                sp.wait_ge(y_copied, t + 1)
                sp.dma_start(out[0, t * P:(t + 1) * P, :], x_io[:, t, :]).then_inc(y_out, 16)
            sp.wait_ge(y_out, 16 * TB)

        @block.tensor
        def _(pe):
            def mm(o, lhs, rhs, start, stop, **kw):
                return nc.tensor.matmul(o, lhs, rhs, start=start, stop=stop, **kw)

            def split_mm(o, terms):
                last = len(terms) - 1
                for n, ((ah, al), (bh, bl)) in enumerate(terms):
                    mm(o, ah, bh, n == 0, False)
                    mm(o, ah, bl, False, False)
                    done = mm(o, al, bh, False, n == last)
                return done

            def w_block(s, k, c, n=W):
                at = k * n + c * P
                return w_hi[:, s, at:at + P], w_lo[:, s, at:at + P]

            def take(s, T, p, U):
                pe.wait_ge(lo_rdy[s], T + 1)
                pe.wait_ge(drained[p], U)

            def wide(s, T, U, r_hi, r_lo):
                take(s, T, s, U)
                for c in range(2):
                    done = split_mm(ps[:, 2 * s + c, :],
                                    [(w_block(s, k, c), (r_hi[:, k, :], r_lo[:, k, :])) for k in range(KB)])
                done.then_inc(tile_done[s], 1)

            def wide_tok(s, T, U):
                take(s, T, s, U)
                for t in range(TB):
                    tok = slice(t * P, (t + 1) * P)
                    done = split_mm(ps[:, 2 * s + t // 2, (t % 2) * W:(t % 2 + 1) * W],
                                    [((h_hi[:, k, tok], h_lo[:, k, tok]),
                                      (w_hi[:, s, k * W:(k + 1) * W], w_lo[:, s, k * W:(k + 1) * W]))
                                     for k in range(KB)])
                done.then_inc(tile_done[s], 1)

            def turn(o, src, n=P):
                return nc.tensor.transpose(o, src, ident[0:n, 0:n])

            def rms_sums(n):
                pe.wait_ge(ssq_rdy, KB * (n + 1))
                pe.wait_ge(rms_sqrt, n)
                mm(ps[:, 4, :], ones[:], sq[:, 1, :], True, True)
                for t in range(TB):
                    done = mm(ps[:, 5, t:t + 1], sq[:, 1, t * P:(t + 1) * P], ones[:, 0:1], True, True)
                done.then_inc(rms_mm, 1)

            pe.wait_ge(const_rdy, CONSTS)
            pe.wait_ge(rows_in, 16)
            turn(ps[:, 7, 0:KB], rows[0:KB, :], KB).then_inc(par_mm, 1)
            pe.wait_ge(x_in, 16)
            for d in range(KB):
                if d == KB - 1:
                    pe.wait_ge(par_rdy, 1)
                for t in range(TB):
                    done = turn(ps[:, d, t * P:(t + 1) * P], x_io[:, t, d * P:(d + 1) * P])
                done.then_inc(x_mm, 1)
            pe.wait_ge(x_copied, KB)
            rms_sums(0)

            def ffn(l, f, t_up, u_up, t_dn, u_dn, norm):
                with pe.Fori(0, NU) as i:
                    pe.wait_ge(h_rdy, KB * norm)
                    for s in range(2):
                        wide(s, l * T_ALL + t_up + i, l * U_ALL + u_up + i, h_hi, h_lo)
                with pe.Fori(0, KB // 2) as i:
                    pe.wait_ge(act_rdy, NU * (2 * l + f + 1))
                    for e in range(2):
                        T = l * T_ALL + t_dn + 2 * i + e
                        for s in range(2):
                            take(s, T, e, l * U_ALL + u_dn + i)
                            for k in range(HK):
                                lh, ll = w_block(s, k, 0, P)
                                f_ = s * HK + k
                                o = ps[:, 2 * e, :]
                                mm(o, lh, act_hi[:, f_, :], f_ == 0, False)
                                mm(o, lh, act_lo[:, f_, :], False, False)
                                done = mm(o, ll, act_hi[:, f_, :], False, f_ == FB - 1)
                            done.then_inc(tile_done[s], 1)
                rms_sums(norm)

            def square_matrix(l, t0, u0, r_hi, r_lo, rdy, value):
                with pe.Fori(0, 2) as i:
                    pe.wait_ge(rdy, value)
                    for s in range(2):
                        wide(s, l * T_ALL + t0 + i, l * U_ALL + u0 + i, r_hi, r_lo)

            def scores(l, i, b):
                n = l * H + 2 * i + b
                pe.wait_ge(k_rdy, l * NJ + i + 1)
                pe.wait_ge(q_rdy, l * NJ + i + 1)
                pe.wait_ge(s_taken, n)
                pe.wait_ge(pt_rdy, n - b if b else n)
                for t in range(TB):
                    tok, keys = slice(t * P, (t + 1) * P), (t + 1) * P
                    o = packed[:, Q_OFF[t]:Q_OFF[t] + keys]
                    mm(o, q_hi[:, b, tok], k_hi[:, b, 0:keys], True, False)
                    mm(o, q_hi[:, b, tok], k_lo[:, b, 0:keys], False, False)
                    mm(o, q_lo[:, b, tok], k_hi[:, b, 0:keys], False, False)
                    done = mm(o[:, keys - P:keys], ident_b[:], causal_b[:], False, True)
                done.then_inc(s_mm, 1)

            def turn_probs(l, i, b):
                n = l * H + 2 * i + b
                pe.wait_ge(p_rdy, n + 1)
                pe.wait_ge(s_taken, l * H + 2 * i + 2)
                pe.wait_ge(pt_rdy, n)
                for t in range(TB):
                    for k in range(t + 1):
                        at = K_OFF[k] + (t - k) * P
                        done = turn(packed[:, at:at + P], prob[:, b, Q_OFF[t] + k * P:Q_OFF[t] + (k + 1) * P])
                done.then_inc(pt_mm, 1)

            def weigh_values(l, i, b):
                n = l * H + 2 * i + b
                pe.wait_ge(pt_rdy, n + 1)
                pe.wait_ge(pv_taken, n)
                for k in range(TB):
                    o = ps[:, 7, k * P:S]
                    cols, at = slice(b * P, (b + 1) * P), slice(K_OFF[k], K_OFF[k] + S - k * P)
                    mm(o, v_hi[:, k, cols], pt_hi[:, at], k == 0, False)
                    mm(o, v_hi[:, k, cols], pt_lo[:, at], False, False)
                    done = mm(o, v_lo[:, k, cols], pt_hi[:, at], False, k == TB - 1)
                done.then_inc(pv_mm, 1)

            def head_sums(n, p, U):
                pe.wait_ge(qk_sq, n + 1)
                pe.wait_ge(drained[p], U)
                for b in range(2):
                    done = mm(ps[:, 2 * p + b, :], ones[:], t_b[:, b, :], True, True)
                done.then_inc(qk_mm, 1)

            def attention_pair(l, i, prev):
                T, U = l * T_ALL + T_C + 2 * i, l * U_ALL + U_C + 3 * i
                n = l * 2 * NJ + 2 * i
                wide(0, T, U, h_hi, h_lo)
                if prev:
                    scores(l, i - 1, 1)
                wide(1, T, U, h_hi, h_lo)
                head_sums(n, 0, U + 1)
                if prev:
                    turn_probs(l, i - 1, 0)
                wide_tok(0, T + 1, U + 2)
                if prev:
                    weigh_values(l, i - 1, 0)
                    turn_probs(l, i - 1, 1)
                head_sums(n + 1, 1, U + 1)
                if prev:
                    weigh_values(l, i - 1, 1)
                wide(1, T + 1, U + 2, h_hi, h_lo)
                scores(l, i, 0)

            with pe.Fori(0, L) as l:
                pe.wait_ge(rows_in, 16 * (7 * l + 8))
                pe.wait_ge(par_rdy, l + 1)
                pe.wait_ge(pv_taken, l * H)
                turn(ps[:, 7, 0:ROWS], rows[0:ROWS, :], ROWS).then_inc(par_mm, 1)
                pe.wait_ge(x_copied, KB)
                ffn(l, 0, T_UP1, U_UP1, T_DN1, U_DN1, 3 * l + 1)

                pe.wait_ge(h_rdy, KB * (3 * l + 2))
                pe.wait_ge(wf_rdy, l + 1)
                for t in range(TB):
                    tok = slice(t * P, (t + 1) * P)
                    done = split_mm(ps[:, 6, t * H:(t + 1) * H],
                                    [((h_hi[:, k, tok], h_lo[:, k, tok]), (wf_hi[:, k, :], wf_lo[:, k, :]))
                                     for k in range(KB)])
                done.then_inc(f_mm, 1)
                with pe.Fori(0, NJ) as i:
                    for s in (0, 1):
                        wide(s, l * T_ALL + T_A + 2 * i, l * U_ALL + U_A + 2 * i, h_hi, h_lo)
                    for s in (0, 1):
                        wide(s, l * T_ALL + T_A + 2 * i + 1, l * U_ALL + U_A + 2 * i + 1, h_hi, h_lo)
                pe.wait_ge(f_rdy, l + 1)
                pe.wait_ge(par_rdy, l + 2)
                for t in range(TB):
                    for j in range(t + 1):
                        m = upper if j == t else ones
                        mm(ps[:, 6, t * H:(t + 1) * H], m[:], lf[:, 0, j, :], j == 0, j == t)
                        done = mm(ps[0:H, 7, t * P:(t + 1) * P], lf[:, 0, j, :], m[:], j == 0, j == t)
                done.then_inc(c_mm, 1)
                square_matrix(l, T_WA, U_WA, br_hi, br_lo, br_rdy, (2 * l + 1) * NJ)

                pe.wait_ge(sw_masked, l + 1)
                pe.wait_ge(rms_sqrt, 3 * l + 2)
                for g in range(H):
                    done = turn(ps[:, 4 + g // 4, (g % 4) * P:(g % 4 + 1) * P], sw_raw[:, g, :])
                done.then_inc(sw_mm, 1)
                with pe.Fori(0, 2) as i:
                    for s in range(2):
                        wide_tok(s, l * T_ALL + T_BV + i, l * U_ALL + U_BV + i)
                with pe.Fori(0, NJ) as i:
                    for s in range(2):
                        wide(s, l * T_ALL + T_BU + i, l * U_ALL + U_BU + i, h_hi, h_lo)
                    pe.wait_ge(sw_rdy, l + 1)
                    pe.wait_ge(vns_rdy, l * NJ + i + 1)
                    pe.wait_ge(sp_added, l * NJ + i)
                    for b in range(2):
                        for t in range(TB):
                            cols = slice(b * P, (b + 1) * P)
                            wh = sw_hi[:, ds(2 * i + b, 1), :].rearrange("p g t -> p (g t)")
                            wl = sw_lo[:, ds(2 * i + b, 1), :].rearrange("p g t -> p (g t)")
                            done = split_mm(ps[:, 4 + b, t * P:(t + 1) * P],
                                            [((vn_hi[:, t, cols], vn_lo[:, t, cols]), (wh, wl))])
                    done.then_inc(sp_mm, 1)
                square_matrix(l, T_WB, U_WB, br_hi, br_lo, br_rdy, (2 * l + 2) * NJ)

                pe.wait_ge(sp_added, (l + 1) * NJ)
                pe.wait_ge(c_copied, 2 * l + 2)
                attention_pair(l, 0, False)
                with pe.Fori(1, NJ) as i:
                    attention_pair(l, i, True)
                scores(l, NJ - 1, 1)
                turn_probs(l, NJ - 1, 0)
                weigh_values(l, NJ - 1, 0)
                turn_probs(l, NJ - 1, 1)
                weigh_values(l, NJ - 1, 1)
                square_matrix(l, T_WC, U_WC, br_hi, br_lo, pv_taken, (l + 1) * H)
                square_matrix(l, T_WO, U_WO, m_hi, m_lo, m_rdy, (l + 1) * NJ)
                rms_sums(3 * l + 2)
                ffn(l, 1, T_UP2, U_UP2, T_DN2, U_DN2, 3 * l + 3)

            pe.wait_ge(rms_sqrt, 3 * L + 1)
            for s in range(2):
                pe.wait_ge(drained[s], L * U_ALL)
            for t in range(TB):
                for d in range(KB):
                    done = turn(ps[:, 2 * t + d // 4, (d % 4) * P:(d % 4 + 1) * P], xT[:, d, t * P:(t + 1) * P])
                done.then_inc(y_mm, 1)

        @block.scalar
        def _(act):
            def copy(o, a, scale=1.0):
                return nc.scalar.activation(o, a, ACT.Copy, scale=scale)

            def split_hi(s, T):
                act.wait_ge(raw_in[s], 16 * (T + 1))
                act.wait_ge(tile_done[s], T)
                copy(w_hi[:, s, :], raw[:, s, :]).then_inc(hi_rdy[s], 1)

            def h_blocks(d, n, r):
                for b in range(n):
                    copy(h_hi[:, ds(d + b, 1), :], xT[:, ds(d + b, 1), :], par[:, ds(r + d + b, 1)]).then_inc(h_hi_rdy, 1)

            def rms_roots(n):
                act.wait_ge(rms_mm, n + 1)
                nc.scalar.activation(rinv[:], ps[:, 4, :], ACT.Sqrt, bias=eps_rms[:], scale=1.0 / D)
                nc.scalar.activation(rtok[:], ps[:, 5, 0:TB], ACT.Sqrt, bias=eps_rms[:],
                                     scale=1.0 / D).then_inc(rms_sqrt, 1)

            def gates(i, br):
                for b in range(2):
                    done = nc.scalar.activation(gate[:, ds(2 * i + b, 1), :], t_b[:, b:b + 1, :], ACT.Sigmoid,
                                                bias=par[:, ds(R_GATE + br * KB + 2 * i + b, 1)])
                done.then_inc(gate_rdy, 1)

            def branch_hi(n, i):
                act.wait_ge(br_prod, n + 1)
                copy(br_hi[:, ds(2 * i, 2), :], t_a[:]).then_inc(br_hi_rdy, 1)

            act.wait_ge(const_rdy, CONSTS)
            act.wait_ge(par_rdy, 1)
            with act.Fori(0, KB) as d:
                act.wait_ge(x_copied, d + 1)
                h_blocks(d, 1, R_NEXT)
            split_hi(0, 0)
            split_hi(1, 0)
            rms_roots(0)

            def ffn(l, f, t_up, u_up, t_dn, u_dn, norm, r):
                with act.Fori(0, NU) as i:
                    T, U, n = l * T_ALL + t_up + i, l * U_ALL + u_up + i, (2 * l + f) * NU + i
                    split_hi(0, T + 1)
                    act.wait_ge(drained[0], U + 1)
                    nc.scalar.activation(t_a[:], t_a[:], ACT.Silu).then_inc(silu_rdy, 1)
                    act.wait_ge(up_prod, n + 1)
                    copy(act_hi[:, ds(2 * i, 2), :], t_b[:]).then_inc(act_hi_rdy, 1)
                    split_hi(1, T + 1)
                with act.Fori(0, KB // 2) as i:
                    for e in range(2):
                        T, U = l * T_ALL + t_dn + 2 * i + e, l * U_ALL + u_dn + i
                        split_hi(0, T + 1)
                        act.wait_ge(drained[e], U + 1)
                        h_blocks(2 * i + e, 1, r)
                        split_hi(1, T + 1)
                rms_roots(norm)

            def plain_tiles(l, t0, count=2):
                with act.Fori(0, count) as i:
                    for s in range(2):
                        split_hi(s, l * T_ALL + t0 + i + 1)

            def exps(l, i, b):
                n = l * H + 2 * i + b
                act.wait_ge(s_max, n + 1)
                for t in range(TB):
                    cols = slice(Q_OFF[t], Q_OFF[t] + (t + 1) * P)
                    done = nc.scalar.activation(prob[:, b, cols], prob[:, b, cols], ACT.Exp,
                                                bias=nmax[:, b, t:t + 1], accum_out=esum[:, b, t:t + 1])
                done.then_inc(s_exp, 1)

            def probs_hi(l, i, b):
                n = l * H + 2 * i + b
                act.wait_ge(pt_mm, n + 1)
                act.wait_ge(pv_mm, n)
                copy(pt_hi[:], packed).then_inc(pt_hi_rdy, 1)

            def heads_hi(l, i, b):
                n = l * H + 2 * i + b
                act.wait_ge(pv_mm, n + 1)
                copy(br_hi[:, ds(2 * i + b, 1), :], ps[:, 7:8, :]).then_inc(pv_hi_rdy, 1)

            def attention_pair(l, i, prev):
                T, U = l * T_ALL + T_C + 2 * i, l * U_ALL + U_C + 3 * i
                n = l * NJ + i
                if prev:
                    exps(l, i - 1, 0)
                split_hi(0, T + 1)
                act.wait_ge(drained[0], U + 1)
                nc.scalar.activation(t_b[:], t_a[:], ACT.Square).then_inc(qk_sq, 1)
                if prev:
                    exps(l, i - 1, 1)
                act.wait_ge(qk_mm, 2 * n + 1)
                nc.scalar.activation(t_b[:], pair(0), ACT.Sqrt, bias=eps_rms[:], scale=1.0 / P).then_inc(drained[0], 1)
                split_hi(1, T + 1)
                act.wait_ge(qk_norm, 2 * n + 1)
                act.wait_ge(s_mm, l * H + 2 * i)
                for b in range(2):
                    done = copy(q_hi[:, b:b + 1, :], t_a[:, b:b + 1, :], par[:, ds(R_Q + 2 * i + b, 1)])
                done.then_inc(q_hi_rdy, 1)
                act.wait_ge(drained[1], U + 1)
                nc.scalar.activation(t_b[:], t_a[:], ACT.Square).then_inc(qk_sq, 1)
                if prev:
                    probs_hi(l, i - 1, 0)
                split_hi(0, T + 2)
                if prev:
                    heads_hi(l, i - 1, 0)
                    probs_hi(l, i - 1, 1)
                act.wait_ge(qk_mm, 2 * n + 2)
                nc.scalar.activation(t_b[:], pair(1), ACT.Sqrt, bias=eps_rms[:], scale=1.0 / P).then_inc(drained[1], 1)
                if prev:
                    heads_hi(l, i - 1, 1)
                act.wait_ge(tile_done[0], T + 2)
                act.wait_ge(pv_mm, l * H + 2 * i)
                for t in range(TB):
                    done = copy(v_hi[:, t, :], ps[:, t // 2, (t % 2) * W:(t % 2 + 1) * W], rtok[:, t:t + 1])
                done.then_inc(v_hi_rdy, 1)
                act.wait_ge(qk_norm, 2 * n + 2)
                for b in range(2):
                    done = copy(k_hi[:, b:b + 1, :], t_a[:, b:b + 1, :], par[:, ds(R_K + 2 * i + b, 1)])
                done.then_inc(k_hi_rdy, 1)
                split_hi(1, T + 2)
                act.wait_ge(drained[1], U + 3)
                gates(i, 2)

            with act.Fori(0, L) as l:
                act.wait_ge(wf_in, 16 * (l + 1))
                act.wait_ge(f_mm, l)
                copy(wf_hi[:], wf_raw[:]).then_inc(wf_hi_rdy, 1)
                ffn(l, 0, T_UP1, U_UP1, T_DN1, U_DN1, 3 * l + 1, R_MIX)

                act.wait_ge(f_steps, 2 * l + 1)
                nc.scalar.activation(lf[:, 2], lf[:, 1], ACT.Exp).then_inc(f_exp, 1)
                act.wait_ge(f_steps, 2 * l + 2)
                nc.scalar.activation(lf[:, 4], lf[:, 3], ACT.Ln).then_inc(f_ln, 1)
                with act.Fori(0, NJ) as i:
                    T, U, n = l * T_ALL + T_A + 2 * i, l * U_ALL + U_A + 2 * i, l * NJ + i
                    split_hi(0, T + 1)
                    split_hi(1, T + 1)
                    act.wait_ge(z_rdy, n + 1)
                    for b in range(2):
                        done = copy(y_c[:, b:b + 1, :], z[:, b:b + 1, 2:S + 2], par[:, ds(R_CONV + 2 * KB + 2 * i + b, 1)])
                    done.then_inc(conv0, 1)
                    split_hi(0, T + 2)
                    branch_hi(2 * l * NJ + i, i)
                    split_hi(1, T + 2)
                    act.wait_ge(drained[1], U + 2)
                    gates(i, 0)
                plain_tiles(l, T_WA)
                act.wait_ge(sw_mm, l + 1)
                copy(sw_hi[:], ps[:, 4:6, :].rearrange("p a (g t) -> p (a g) t", t=P)).then_inc(sw_hi_rdy, 1)
                act.wait_ge(rms_rdy, 3 * l + 2)
                act.wait_ge(c_out, 16 * (l + 1))
                with act.Fori(0, 2) as i:
                    for s in range(2):
                        T = l * T_ALL + T_BV + i
                        split_hi(s, T + 1)
                        for t in range(TB):
                            done = nc.scalar.activation(
                                vn[:, t, ds((2 * i + s) * W, W)], ps[:, 2 * s + t // 2, (t % 2) * W:(t % 2 + 1) * W],
                                ACT.Gelu, scale=rtok[:, t:t + 1])
                        done.then_inc(drained[s], 1)
                act.wait_ge(ln_mv, l + 1)
                nc.scalar.activation(rstd[:], mv[:, :, 1], ACT.Sqrt, bias=eps_ln[:]).then_inc(ln_sqrt, 1)
                with act.Fori(0, NJ) as i:
                    T, U, n = l * T_ALL + T_BU + i, l * U_ALL + U_BU + i, l * NJ + i
                    split_hi(0, T + 1)
                    act.wait_ge(drained[0], U + 1)
                    nc.scalar.activation(t_a[:], t_a[:], ACT.Gelu).then_inc(gelu_rdy, 1)
                    act.wait_ge(vn_rdy, TB * (l + 1))
                    act.wait_ge(sp_mm, n)
                    copy(vn_hi[:], vn[:, :, ds(i * W, W)]).then_inc(vn_hi_rdy, 1)
                    split_hi(1, T + 1)
                    act.wait_ge(drained[1], U + 1)
                    gates(i, 1)
                    branch_hi((2 * l + 1) * NJ + i, i)
                plain_tiles(l, T_WB)
                attention_pair(l, 0, False)
                with act.Fori(1, NJ) as i:
                    attention_pair(l, i, True)
                for b in range(2):
                    exps(l, NJ - 1, b)
                for b in range(2):
                    probs_hi(l, NJ - 1, b)
                    heads_hi(l, NJ - 1, b)
                with act.Fori(0, 2) as i:
                    for s in range(2):
                        split_hi(s, l * T_ALL + T_WC + i + 1)
                        act.wait_ge(mg_add, 8 * l + 4 + 2 * i + s + 1)
                        copy(m_hi[:, ds(4 * i + 2 * s, 2), :], (t_a, t_b)[s][:]).then_inc(m_hi_rdy, 1)
                with act.Fori(0, 2) as i:
                    for s in range(2):
                        split_hi(s, l * T_ALL + T_WO + i + 1)
                        act.wait_ge(drained[s], l * U_ALL + U_WO + i + 1)
                        h_blocks(4 * i + 2 * s, 2, R_FFN2)
                rms_roots(3 * l + 2)
                ffn(l, 1, T_UP2, U_UP2, T_DN2, U_DN2, 3 * l + 3, R_NEXT)
            for t in (1, 3):
                act.wait_ge(y_mm, t + 1)
                act.wait_ge(y_copied, t)
                copy(x_io[:, t, :], ps[:, 2 * t:2 * t + 2, :].rearrange("p a s -> p (a s)")).then_inc(y_copied, 1)

        @block.vector
        def _(dve):
            V = nc.vector

            def split_lo(s, T):
                dve.wait_ge(hi_rdy[s], T + 1)
                V.tensor_tensor(w_lo[:, s, :], raw[:, s, :], w_hi[:, s, :].bitcast(F32), ALU.subtract).then_inc(lo_rdy[s], 1)

            def h_blocks(d, n, r, count):
                dve.wait_ge(h_hi_rdy, count)
                for b in range(n):
                    V.scalar_tensor_tensor(
                        out=h_lo[:, ds(d + b, 1), :], in0=xT[:, ds(d + b, 1), :], scalar=par[:, ds(r + d + b, 1)],
                        in1=h_hi[:, ds(d + b, 1), :].bitcast(F32), op0=ALU.mult,
                        op1=ALU.subtract).then_inc(h_rdy, 1)

            def rms_inverse(n):
                dve.wait_ge(rms_sqrt, n + 1)
                V.reciprocal(rinv[:], rinv[:])
                V.reciprocal(rtok[:], rtok[:]).then_inc(rms_rdy, 1)

            def take(p, T, U, dst):
                dve.wait_ge(tile_done[p], T + 1)
                V.tensor_tensor(dst[:], pair(p), over_pair(rinv[:]), ALU.mult).then_inc(drained[p], 1)

            def branch_lo(n, i):
                dve.wait_ge(br_hi_rdy, n + 1)
                V.tensor_tensor(br_lo[:, ds(2 * i, 2), :], t_a[:], br_hi[:, ds(2 * i, 2), :].bitcast(F32),
                                ALU.subtract).then_inc(br_rdy, 1)

            dve.wait_ge(par_mm, 1)
            V.tensor_copy(par[:, R_NEXT:R_NEXT + KB], ps[:, 7, 0:KB]).then_inc(par_rdy, 1)
            with dve.Fori(0, KB) as d:
                dve.wait_ge(x_mm, d + 1)
                V.tensor_copy(xT[:, ds(d, 1), :], ps[:, ds(d, 1), :]).then_inc(x_copied, 1)
                dve.wait_ge(x_copied, d + 1)
                h_blocks(d, 1, R_NEXT, d + 1)
            split_lo(0, 0)
            split_lo(1, 0)
            rms_inverse(0)

            def ffn(l, f, t_up, u_up, t_dn, u_dn, norm, r):
                with dve.Fori(0, NU) as i:
                    T, U, n = l * T_ALL + t_up + i, l * U_ALL + u_up + i, (2 * l + f) * NU + i
                    dve.wait_ge(rms_rdy, norm)
                    take(0, T, U, t_a)
                    split_lo(0, T + 1)
                    take(1, T, U, t_b)
                    dve.wait_ge(silu_rdy, n + 1)
                    dve.wait_ge(drained[1], U + 1)
                    V.tensor_tensor(t_b[:], t_a[:], t_b[:], ALU.mult).then_inc(up_prod, 1)
                    dve.wait_ge(act_hi_rdy, n + 1)
                    V.tensor_tensor(act_lo[:, ds(2 * i, 2), :], t_b[:], act_hi[:, ds(2 * i, 2), :].bitcast(F32),
                                    ALU.subtract).then_inc(act_rdy, 1)
                    split_lo(1, T + 1)
                with dve.Fori(0, KB // 2) as i:
                    for e in range(2):
                        T, U, d = l * T_ALL + t_dn + 2 * i + e, l * U_ALL + u_dn + i, 2 * i + e
                        split_lo(0, T + 1)
                        dve.wait_ge(tile_done[1], T + 1)
                        V.scalar_tensor_tensor(out=xT[:, ds(d, 1), :], in0=ps[:, 2 * e:2 * e + 1, :], scalar=0.5,
                                               in1=xT[:, ds(d, 1), :], op0=ALU.mult, op1=ALU.add).then_inc(drained[e], 1)
                        dve.wait_ge(drained[e], U + 1)
                        h_blocks(d, 1, r, KB * norm + d + 1)
                        split_lo(1, T + 1)
                rms_inverse(norm)

            def softmax_head(l, i, b):
                n = l * H + 2 * i + b
                dve.wait_ge(s_mm, n + 1)
                dve.wait_ge(cn_in, 16 * (l * NJ + i + 1))
                for t in range(TB):
                    keys = (t + 1) * P
                    cols = slice(Q_OFF[t], Q_OFF[t] + keys)
                    done = V.scalar_tensor_tensor(
                        out=prob[:, b, cols], in0=cn_bc[:, b, 0:keys],
                        scalar=c_tok[:, t, ds(2 * i + b, 1)], in1=packed[:, cols],
                        op0=ALU.add, op1=ALU.add)
                done.then_inc(s_taken, 1)
                dve.wait_ge(s_taken, n + 1)
                for t in range(TB):
                    done = V.tensor_reduce(nmax[:, b, t:t + 1], prob[:, b, Q_OFF[t]:Q_OFF[t] + (t + 1) * P],
                                           AX_X, ALU.max, negate=True)
                done.then_inc(s_max, 1)

            def softmax_scale(l, i, b):
                n = l * H + 2 * i + b
                dve.wait_ge(s_exp, n + 1)
                V.reciprocal(esum[:, b, :], esum[:, b, :]).then_inc(s_rcp, 1)
                dve.wait_ge(s_rcp, n + 1)
                for t in range(TB):
                    cols = slice(Q_OFF[t], Q_OFF[t] + (t + 1) * P)
                    done = V.tensor_scalar(prob[:, b, cols], prob[:, b, cols], esum[:, b, t:t + 1], None, ALU.mult)
                done.then_inc(p_rdy, 1)

            def probs_lo(l, i, b):
                n = l * H + 2 * i + b
                dve.wait_ge(pt_hi_rdy, n + 1)
                V.tensor_tensor(pt_lo[:], packed, pt_hi[:].bitcast(F32), ALU.subtract).then_inc(pt_rdy, 1)

            def heads_lo(l, i, b):
                n = l * H + 2 * i + b
                dve.wait_ge(pv_hi_rdy, n + 1)
                V.tensor_tensor(br_lo[:, ds(2 * i + b, 1), :], ps[:, 7:8, :],
                                br_hi[:, ds(2 * i + b, 1), :].bitcast(F32), ALU.subtract).then_inc(pv_taken, 1)

            def normalized(n):
                V.reciprocal(t_b[:], t_b[:]).then_inc(qk_inv, 1)
                dve.wait_ge(qk_inv, n + 1)
                V.tensor_tensor(t_a[:], t_a[:], t_b[:], ALU.mult).then_inc(qk_norm, 1)

            def gained_lo(o_hi, o_lo, r, i, hi_sem, n, rdy):
                dve.wait_ge(hi_sem, n + 1)
                for b in range(2):
                    done = V.scalar_tensor_tensor(out=o_lo[:, b:b + 1, :], in0=t_a[:, b:b + 1, :],
                                                  scalar=par[:, ds(r + 2 * i + b, 1)],
                                                  in1=o_hi[:, b:b + 1, :].bitcast(F32),
                                                  op0=ALU.mult, op1=ALU.subtract)
                done.then_inc(rdy, 1)

            def attention_pair(l, i, prev):
                T, U = l * T_ALL + T_C + 2 * i, l * U_ALL + U_C + 3 * i
                n = l * NJ + i
                if prev:
                    softmax_head(l, i - 1, 0)
                    softmax_scale(l, i - 1, 0)
                dve.wait_ge(k_rdy, n)
                dve.wait_ge(mg_add, 8 * l + 4)
                take(0, T, U, t_a)
                split_lo(0, T + 1)
                if prev:
                    softmax_head(l, i - 1, 1)
                    softmax_scale(l, i - 1, 1)
                dve.wait_ge(drained[0], U + 2)
                normalized(2 * n)
                gained_lo(q_hi, q_lo, R_Q, i, q_hi_rdy, n, q_rdy)
                dve.wait_ge(q_rdy, n + 1)
                take(1, T, U, t_a)
                split_lo(1, T + 1)
                if prev:
                    probs_lo(l, i - 1, 0)
                split_lo(0, T + 2)
                if prev:
                    heads_lo(l, i - 1, 0)
                    probs_lo(l, i - 1, 1)
                dve.wait_ge(drained[1], U + 2)
                normalized(2 * n + 1)
                if prev:
                    heads_lo(l, i - 1, 1)
                dve.wait_ge(v_hi_rdy, n + 1)
                for t in range(TB):
                    done = V.scalar_tensor_tensor(
                        out=v_lo[:, t, :], in0=ps[:, t // 2, (t % 2) * W:(t % 2 + 1) * W], scalar=rtok[:, t:t + 1],
                        in1=v_hi[:, t, :].bitcast(F32), op0=ALU.mult, op1=ALU.subtract)
                done.then_inc(drained[0], 1)
                gained_lo(k_hi, k_lo, R_K, i, k_hi_rdy, n, k_rdy)
                dve.wait_ge(qk_norm, 2 * n + 2)
                take(1, T + 1, U + 2, t_b)
                split_lo(1, T + 2)

            with dve.Fori(0, L) as l:
                dve.wait_ge(par_mm, l + 2)
                dve.wait_ge(h_rdy, KB * (3 * l + 1))
                V.tensor_copy(par[:, 0:R_Q], ps[:, 7, 0:R_Q])
                V.tensor_scalar(par[:, R_Q:R_Q + KB], ps[:, 7, R_Q:R_Q + KB], SC, None, ALU.mult)
                V.tensor_copy(par[:, R_K:ROWS], ps[:, 7, R_K:ROWS]).then_inc(par_rdy, 1)
                dve.wait_ge(par_rdy, l + 2)
                dve.wait_ge(wf_hi_rdy, l + 1)
                V.tensor_tensor(wf_lo[:], wf_raw[:], wf_hi[:].bitcast(F32), ALU.subtract).then_inc(wf_rdy, 1)
                ffn(l, 0, T_UP1, U_UP1, T_DN1, U_DN1, 3 * l + 1, R_MIX)

                def step(k, ins):
                    ins.then_inc(f_chain, 1)
                    dve.wait_ge(f_chain, 7 * l + k)

                dve.wait_ge(rms_rdy, 3 * l + 2)
                dve.wait_ge(f_mm, l + 1)
                dve.wait_ge(bf_in, 16 * (l + 1))
                step(1, V.tensor_tensor(lf[:, 0], ps[:, 6, 0:TB * H].rearrange("p (t h) -> p t h", h=H),
                                        rtok[:].unsqueeze(2).broadcast_to([P, TB, H]), ALU.mult))
                step(2, V.tensor_tensor(lf[:, 0], lf[:, 0], bf_bc[:].unsqueeze(1).broadcast_to([P, TB, H]), ALU.add))
                V.scalar_tensor_tensor(out=lf[:, 1], in0=lf[:, 0], scalar=-1.0, in1=lf[:, 0],
                                       op0=ALU.mult, op1=ALU.min).then_inc(f_steps, 1)
                dve.wait_ge(f_exp, l + 1)
                V.tensor_scalar(lf[:, 3], lf[:, 2], 1.0, None, ALU.add).then_inc(f_steps, 1)
                dve.wait_ge(f_steps, 2 * l + 2)
                step(3, V.scalar_tensor_tensor(out=lf[:, 2], in0=lf[:, 3], scalar=-1.0, in1=lf[:, 2],
                                               op0=ALU.add, op1=ALU.subtract))
                step(4, V.reciprocal(lf[:, 5], lf[:, 3]))
                step(5, V.tensor_tensor(lf[:, 2], lf[:, 2], lf[:, 5], ALU.mult))
                dve.wait_ge(f_ln, l + 1)
                step(6, V.scalar_tensor_tensor(out=lf[:, 0], in0=lf[:, 0], scalar=0.0, in1=lf[:, 4],
                                               op0=ALU.min, op1=ALU.subtract))
                step(7, V.tensor_tensor(lf[:, 0], lf[:, 0], lf[:, 2], ALU.add))
                V.memset(z[:, :, 0:2], 0.0).then_inc(f_rdy, 1)
                with dve.Fori(0, NJ) as i:
                    T, U, n = l * T_ALL + T_A + 2 * i, l * U_ALL + U_A + 2 * i, l * NJ + i
                    dve.wait_ge(f_rdy, l + 1)
                    dve.wait_ge(br_rdy, 2 * l * NJ + i)
                    take(0, T, U, t_a)
                    split_lo(0, T + 1)
                    dve.wait_ge(gate_rdy, 3 * l * NJ + i)
                    take(1, T, U, t_b)
                    dve.wait_ge(drained[1], U + 1)
                    V.tensor_tensor(z[:, :, 2:S + 2], t_a[:], t_b[:], ALU.mult).then_inc(z_rdy, 1)
                    split_lo(1, T + 1)
                    for tap, before, after in ((1, conv0, conv1), (0, conv1, conv2)):
                        dve.wait_ge(before, n + 1)
                        for b in range(2):
                            done = V.scalar_tensor_tensor(
                                out=y_c[:, b:b + 1, :], in0=z[:, b:b + 1, tap:tap + S],
                                scalar=par[:, ds(R_CONV + tap * KB + 2 * i + b, 1)], in1=y_c[:, b:b + 1, :],
                                op0=ALU.mult, op1=ALU.add)
                        done.then_inc(after, 1)
                    dve.wait_ge(tile_done[0], T + 2)
                    V.tensor_tensor(t_a[:], pair(0), over_pair(rinv[:]), ALU.mult).then_inc(drained[0], 1)
                    dve.wait_ge(drained[0], U + 2)
                    dve.wait_ge(conv2, n + 1)
                    V.tensor_tensor(t_a[:], t_a[:], y_c[:], ALU.mult).then_inc(br_prod, 1)
                    split_lo(0, T + 2)
                    branch_lo(2 * l * NJ + i, i)
                    take(1, T + 1, U + 1, t_b)
                    split_lo(1, T + 2)
                dve.wait_ge(c_mm, l + 1)
                V.tensor_copy(c_tok[:], ps[:, 6, 0:TB * H].rearrange("p (t h) -> p t h", h=H)).then_inc(c_copied, 1)
                dve.wait_ge(c_out, 16 * l)
                V.tensor_scalar(c_neg[:], ps[0:H, 7, :], -1.0, None, ALU.mult).then_inc(c_copied, 1)
                with dve.Fori(0, 2) as i:
                    for s in range(2):
                        dve.wait_ge(gate_rdy, (3 * l + 1) * NJ)
                        T = l * T_ALL + T_WA + i
                        d = 4 * i + 2 * s
                        dve.wait_ge(tile_done[s], T + 1)
                        V.tensor_tensor(merged[:, ds(d, 2), :], pair(s), gate[:, ds(d, 2), :], ALU.mult).then_inc(drained[s], 1)
                        split_lo(s, T + 1)
                with dve.Fori(0, 2) as i:
                    for s in range(2):
                        split_lo(s, l * T_ALL + T_BV + i + 1)
                for s in range(2):
                    dve.wait_ge(drained[s], l * U_ALL + U_BU)
                for t in range(TB):
                    for c in range(2):
                        done = V.bn_stats(stats[:, t, c, :], vn[:, t, c * S:(c + 1) * S])
                done.then_inc(ln_stats, 1)
                dve.wait_ge(ln_stats, l + 1)
                dve.wait_ge(sw_hi_rdy, l + 1)
                V.tensor_tensor(sw_lo[:], ps[:, 4:6, :].rearrange("p a (g t) -> p (a g) t", t=P),
                                sw_hi[:].bitcast(F32), ALU.subtract).then_inc(sw_rdy, 1)
                for t in range(TB):
                    done = V.bn_aggr(mv[:, t, :], stats[:, t, :, :].rearrange("p c k -> p (c k)"))
                done.then_inc(ln_mv, 1)
                dve.wait_ge(ln_sqrt, l + 1)
                V.reciprocal(rstd[:], rstd[:]).then_inc(ln_rstd, 1)
                dve.wait_ge(ln_rstd, l + 1)
                for t in range(TB):
                    V.tensor_scalar(vn[:, t, :], vn[:, t, :], mv[:, t, 0:1], rstd[:, t:t + 1],
                                    ALU.subtract, ALU.mult).then_inc(ln_norm, 1)

                with dve.Fori(0, NJ) as i:
                    T, U, n = l * T_ALL + T_BU + i, l * U_ALL + U_BU + i, l * NJ + i
                    dve.wait_ge(br_rdy, (2 * l + 1) * NJ + i)
                    take(0, T, U, t_a)
                    split_lo(0, T + 1)
                    dve.wait_ge(vn_hi_rdy, n + 1)
                    V.tensor_tensor(vn_lo[:], vn[:, :, ds(i * W, W)], vn_hi[:].bitcast(F32), ALU.subtract).then_inc(vns_rdy, 1)
                    dve.wait_ge(gate_rdy, (3 * l + 1) * NJ + i)
                    take(1, T, U, t_b)
                    split_lo(1, T + 1)
                    dve.wait_ge(sp_mm, n + 1)
                    for b in range(2):
                        done = V.tensor_tensor(
                            y_c[:, b, :].rearrange("p (t s) -> p t s", s=P), ps[:, 4 + b, :].rearrange("p (t s) -> p t s", s=P),
                            bs_bc[:, ds(2 * i + b, 1), :].broadcast_to([P, TB, P]), ALU.add)
                    done.then_inc(sp_added, 1)
                    dve.wait_ge(sp_added, n + 1)
                    dve.wait_ge(gelu_rdy, n + 1)
                    V.tensor_tensor(t_a[:], t_a[:], y_c[:], ALU.mult).then_inc(br_prod, 1)
                    branch_lo((2 * l + 1) * NJ + i, i)
                with dve.Fori(0, 2) as i:
                    for s in range(2):
                        dve.wait_ge(gate_rdy, (3 * l + 2) * NJ)
                        T, U, t = l * T_ALL + T_WB + i, l * U_ALL + U_WB + i, (t_a, t_b)[s]
                        dve.wait_ge(br_rdy, (2 * l + 2) * NJ)
                        dve.wait_ge(mg_add, 8 * l + 2 * i)
                        d = 4 * i + 2 * s
                        dve.wait_ge(tile_done[s], T + 1)
                        V.tensor_tensor(t[:], pair(s), gate[:, ds(d, 2), :], ALU.mult).then_inc(drained[s], 1)
                        dve.wait_ge(drained[s], U + 1)
                        V.tensor_tensor(merged[:, ds(d, 2), :], merged[:, ds(d, 2), :], t[:], ALU.add).then_inc(mg_add, 1)
                        split_lo(s, T + 1)
                attention_pair(l, 0, False)
                with dve.Fori(1, NJ) as i:
                    attention_pair(l, i, True)
                for b in range(2):
                    softmax_head(l, NJ - 1, b)
                    softmax_scale(l, NJ - 1, b)
                for b in range(2):
                    probs_lo(l, NJ - 1, b)
                    heads_lo(l, NJ - 1, b)
                with dve.Fori(0, 2) as i:
                    for s in range(2):
                        dve.wait_ge(gate_rdy, (3 * l + 3) * NJ)
                        T, U, t = l * T_ALL + T_WC + i, l * U_ALL + U_WC + i, (t_a, t_b)[s]
                        d, n = 4 * i + 2 * s, 4 * l + 2 * i + s
                        dve.wait_ge(k_rdy, (l + 1) * NJ)
                        dve.wait_ge(m_rdy, 4 * l + 2 * i)
                        dve.wait_ge(tile_done[s], T + 1)
                        V.tensor_tensor(t[:], pair(s), gate[:, ds(d, 2), :], ALU.mult).then_inc(drained[s], 1)
                        dve.wait_ge(drained[s], U + 1)
                        V.tensor_tensor(t[:], merged[:, ds(d, 2), :], t[:], ALU.add).then_inc(mg_add, 1)
                        dve.wait_ge(m_hi_rdy, n + 1)
                        V.tensor_tensor(m_lo[:, ds(d, 2), :], t[:], m_hi[:, ds(d, 2), :].bitcast(F32),
                                        ALU.subtract).then_inc(m_rdy, 1)
                        split_lo(s, T + 1)
                with dve.Fori(0, 2) as i:
                    for s in range(2):
                        T, U, d = l * T_ALL + T_WO + i, l * U_ALL + U_WO + i, 4 * i + 2 * s
                        dve.wait_ge(tile_done[s], T + 1)
                        V.tensor_tensor(xT[:, ds(d, 2), :], pair(s), xT[:, ds(d, 2), :], ALU.add).then_inc(drained[s], 1)
                        dve.wait_ge(drained[s], U + 1)
                        h_blocks(d, 2, R_FFN2, KB * (3 * l + 2) + d + 2)
                        split_lo(s, T + 1)
                rms_inverse(3 * l + 2)
                ffn(l, 1, T_UP2, U_UP2, T_DN2, U_DN2, 3 * l + 3, R_NEXT)
            for t in (0, 2):
                dve.wait_ge(y_mm, t + 1)
                dve.wait_ge(y_copied, t)
                V.tensor_copy(x_io[:, t, :], ps[:, 2 * t:2 * t + 2, :].rearrange("p a s -> p (a s)")).then_inc(y_copied, 1)

        @block.gpsimd
        def _(pool):
            G = nc.gpsimd

            def causal(m, op, fill, step, chan):
                G.affine_select(out=m[:], in_=m[:], compare_op=op, fill=fill, base=0,
                                pattern=[[step, P]], channel_multiplier=chan).then_inc(const_rdy, 1)

            G.memset(eps_rms[:], RMS_EPS)
            G.memset(eps_ln[:], LN_EPS)
            G.memset(ones[:], 1.0)
            G.memset(ident[:], 0.0)
            G.memset(ident_b[:], 0.0)
            G.memset(causal_b[:], 0.0)
            G.memset(lower[:], 1.0)
            G.memset(upper[:], 1.0).then_inc(const_rdy, 1)
            pool.wait_ge(const_rdy, 1)
            causal(ident, ALU.not_equal, 1.0, -1, 1)
            causal(ident_b, ALU.not_equal, 1.0, -1, 1)
            causal(causal_b, ALU.is_ge, MASKED, -1, 1)
            causal(upper, ALU.is_ge, 0.0, 1, -1)
            causal(lower, ALU.is_ge, 0.0, -1, 1)

            def first_square(n):
                pool.wait_ge(rms_mm, n)
                G.tensor_tensor(sq[:, 1, :], xT[:, 0, :], xT[:, 0, :], ALU.mult).then_inc(ssq_rdy, 1)

            def squares(n, d):
                pool.wait_ge(ssq_rdy, KB * n + d)
                G.tensor_tensor(sq[:, 0:1, :], xT[:, ds(d, 1), :], xT[:, ds(d, 1), :], ALU.mult).then_inc(sq_rdy, 1)
                pool.wait_ge(sq_rdy, (KB - 1) * n + d)
                G.tensor_tensor(sq[:, 1:2, :], sq[:, 1:2, :], sq[:, 0:1, :], ALU.add).then_inc(ssq_rdy, 1)

            pool.wait_ge(x_copied, 1)
            first_square(0)
            with pool.Fori(1, KB) as d:
                pool.wait_ge(x_copied, d + 1)
                squares(0, d)

            def ffn(l, u_dn, norm):
                pool.wait_ge(drained[0], l * U_ALL + u_dn + 1)
                first_square(norm)
                pool.wait_ge(drained[1], l * U_ALL + u_dn + 1)
                squares(norm, 1)
                with pool.Fori(1, KB // 2) as i:
                    for e in range(2):
                        pool.wait_ge(drained[e], l * U_ALL + u_dn + i + 1)
                        squares(norm, 2 * i + e)

            with pool.Fori(0, L) as l:
                ffn(l, U_DN1, 3 * l + 1)
                pool.wait_ge(sw_in, 16 * (l + 1))
                pool.wait_ge(const_rdy, CONSTS)
                G.tensor_tensor(sw_raw[:], sw_raw[:], lower[:].unsqueeze(1).broadcast_to([P, H, P]),
                                ALU.mult).then_inc(sw_masked, 1)
                pool.wait_ge(lng_in, 16 * (l + 1))
                pool.wait_ge(lnb_in, 16 * (l + 1))
                for t in range(TB):
                    pool.wait_ge(ln_norm, TB * l + t + 1)
                    G.tensor_tensor(vn[:, t, :], vn[:, t, :], ln_g, ALU.mult).then_inc(ln_gained, 1)
                    pool.wait_ge(ln_gained, TB * l + t + 1)
                    G.tensor_tensor(vn[:, t, :], vn[:, t, :], ln_b, ALU.add).then_inc(vn_rdy, 1)
                pool.wait_ge(s_taken, (l + 1) * H)
                pool.wait_ge(drained[0], l * U_ALL + U_WO + 1)
                first_square(3 * l + 2)
                squares(3 * l + 2, 1)
                pool.wait_ge(drained[1], l * U_ALL + U_WO + 1)
                squares(3 * l + 2, 2)
                squares(3 * l + 2, 3)
                with pool.Fori(1, 2) as i:
                    for s in range(2):
                        pool.wait_ge(drained[s], l * U_ALL + U_WO + i + 1)
                        for b in range(2):
                            squares(3 * l + 2, 4 * i + 2 * s + b)
                ffn(l, U_DN2, 3 * l + 3)


_INS = ["x", "ffn1_norm", "ffn1_w_gu", "ffn1_w_down", "mix_norm", "w_in", "b_forget", "b_gate", "conv_w",
        "sgu_ln_g", "sgu_ln_b", "sgu_w", "sgu_b", "q_norm_g", "k_norm_g", "w_out_conv", "w_out_sgu",
        "w_out_attn", "w_o", "ffn2_norm", "ffn2_w_gu", "ffn2_w_down"]


def kernel(**inputs):
    import numpy as _np
    import concourse.bacc as _bacc
    from concourse.bass_utils import run_bass_kernel_spmd as _run

    nc = _bacc.Bacc("TRN2", target_bir_lowering=False, num_devices=1, dynamic_dma_scratch_size=1024)
    arrays, args = {}, []
    for name in _INS:
        a = _np.ascontiguousarray(inputs[name])
        arrays[f"in_{name}_dram"] = a
        args.append(nc.dram_tensor(f"in_{name}_dram", a.shape, mybir.dt.from_np(a.dtype), kind="ExternalInput").ap())
    out = nc.dram_tensor("out_0_dram", inputs["x"].shape, F32, kind="ExternalOutput").ap()
    build(nc, *args, out)
    r = _run(nc, [arrays], core_ids=[0])
    return r.results[0]["out_0_dram"]
```

```python
from contextlib import ExitStack

import concourse.bass as bass
from concourse import mybir

ALU = mybir.AluOpType
ACT = mybir.ActivationFunctionType
AX_X = mybir.AxisListType.X
F32 = mybir.dt.float32
F32R = mybir.dt.float32r
BF16 = mybir.dt.bfloat16

P = 128
RMS_EPS = 1e-6
LN_EPS = 1e-5
MASKED = -1e30


def ds(start, n):
    return bass.ds(start, n)


def build(nc, x, ffn1_norm, ffn1_w_gu, ffn1_w_down, mix_norm, w_in, b_forget, b_gate, conv_w,
          sgu_ln_g, sgu_ln_b, sgu_w, sgu_b, q_norm_g, k_norm_g, w_out_conv, w_out_sgu,
          w_out_attn, w_o, ffn2_norm, ffn2_w_gu, ffn2_w_down, out):
    L, D, _ = ffn1_w_gu.shape
    S = x.shape[1]
    FF = ffn1_w_down.shape[1]
    H = b_forget.shape[1]
    KB = D // P
    FB = FF // P
    TB = S // P
    W = 2 * P
    NJ = D // W
    NU = FF // W
    HK = FB // 2
    CELLS = KB * W
    SC = float(P) ** -0.5
    assert H == KB and x.shape[0] == 1 and NJ == 4 and TB == 4 and D == 2 * S
    assert FB % 2 == 0 and HK * P <= CELLS

    C_B, C_C, C_X, C_SU, C_SV, C_Q, C_K, C_V = (n * D for n in range(8))
    C_F = 8 * D
    C_G = C_F + H

    T_UP1, T_DN1, T_A, T_BV, T_WA, T_BU, T_WB, T_C, T_WC, T_WO, T_UP2, T_DN2, T_ALL = (
        0, NU, NU + KB, NU + KB + 8, NU + KB + 10, NU + KB + 12, NU + KB + 16, NU + KB + 18,
        NU + KB + 26, NU + KB + 28, NU + KB + 30, 2 * NU + KB + 30, 2 * NU + 2 * KB + 30)
    U_UP1, U_DN1, U_A, U_BV, U_WA, U_BU, U_WB, U_C, U_WC, U_WO, U_UP2, U_DN2, U_ALL = (
        0, NU, NU + NJ, NU + NJ + 8, NU + NJ + 10, NU + NJ + 12, NU + NJ + 16, NU + NJ + 18,
        NU + NJ + 30, NU + NJ + 32, NU + NJ + 34, 2 * NU + NJ + 34, 2 * NU + 2 * NJ + 34)

    CONSTS = 6

    R_MIX, R_CONV, R_GATE, R_Q, R_K, R_FFN2, R_NEXT = 0, KB, 4 * KB, 7 * KB, 8 * KB, 9 * KB, 10 * KB
    ROWS = 11 * KB

    Q_OFF = [896, 1024, 512, 0]
    K_OFF = [0, 512, 1024, 896]
    PACKED = 1280

    with ExitStack() as ctx:
        def sem(name):
            return ctx.enter_context(nc.semaphore(name))

        def sb(name, shape, dt=F32, stack=ctx):
            return stack.enter_context(nc.sbuf_tensor(name, shape, dt))

        ps = ctx.enter_context(nc.psum_tensor("ps", [P, 8, S], F32))
        ps_flat = ps[:].rearrange("p b s -> p (b s)")
        packed = ps_flat[:, 4 * S:4 * S + PACKED]

        xT = sb("xT", [P, KB, S])
        h_hi = sb("h_hi", [P, KB, S], F32R)
        h_lo = sb("h_lo", [P, KB, S], F32R)
        raw = sb("raw", [P, 2, CELLS])
        w_hi = sb("w_hi", [P, 2, CELLS], F32R)
        w_lo = sb("w_lo", [P, 2, CELLS], F32R)
        rinv = sb("rinv", [P, S])
        rtok = sb("rtok", [P, TB])
        t_a = sb("t_a", [P, 2, S])
        t_b = sb("t_b", [P, 2, S])
        sq = sb("sq", [P, 2, S])
        y_c = sq
        cn_bc = sq
        ident = sb("ident", [P, P])
        ident_b = sb("ident_b", [P, P], BF16)
        causal_b = sb("causal_b", [P, P], BF16)
        upper = sb("upper", [P, P])
        lower = sb("lower", [P, P])
        ones = sb("ones", [P, P])
        rows = sb("rows", [P, P])
        par = sb("par", [P, ROWS])
        wf_raw = sb("wf_raw", [P, KB, H])
        wf = sb("wf", [P, KB, H])
        bf_bc = sb("bf_bc", [P, H])
        c_tok = sb("c_tok", [P, TB, H])
        hsum = sb("hsum", [P, 2 * TB])
        hscale = sb("hscale", [P, 2 * TB])
        nmax = sb("nmax", [P, 2, TB])
        esum = sb("esum", [P, 2, TB])
        stats = sb("stats", [P, TB, 2, 6])
        mv = sb("mv", [P, TB, 2])
        rstd = sb("rstd", [P, TB])
        eps_rms = sb("eps_rms", [P, 1])
        eps_ln = sb("eps_ln", [P, 1])
        c_dram = nc.dram_tensor("c_scratch", (H, S), F32, kind="Internal").ap()

        with ExitStack() as ffn:
            act_hi = sb("act_hi", [P, FB, S], F32R, ffn)
            act_lo = sb("act_lo", [P, FB, S], F32R, ffn)
        with ExitStack() as ends:
            x_io = sb("x_io", [P, TB, D], F32, ends)
        br_hi = sb("br_hi", [P, KB, S], F32R)
        br_lo = sb("br_lo", [P, KB, S], F32R)
        gate = sb("gate", [P, KB, S])
        merged = sb("merged", [P, KB, S])
        with ExitStack() as b_mem:
            sw_raw = sb("sw_raw", [P, H, P], F32, b_mem)
            bs_bc = sb("bs_bc", [P, H, P], F32, b_mem)
            with ExitStack() as a_mem:
                z = sb("z", [P, 2, S + 2], F32, a_mem)
            vn = sb("vn", [P, TB, D], F32, b_mem)
            vn_hi = sb("vn_hi", [P, TB, W], F32R, b_mem)
            vn_lo = sb("vn_lo", [P, TB, W], F32R, b_mem)
            sw_hi = sb("sw_hi", [P, H, P], F32R, b_mem)
            sw_lo = sb("sw_lo", [P, H, P], F32R, b_mem)
            c_neg = sb("c_neg", [H, S], F32, b_mem)
            lf = sb("lf", [P, 6, TB, H], F32, b_mem)
        with ExitStack() as c_mem:
            q_hi = sb("q_hi", [P, 2, S], F32R, c_mem)
            q_lo = sb("q_lo", [P, 2, S], F32R, c_mem)
            k_hi = sb("k_hi", [P, 2, S], F32R, c_mem)
            k_lo = sb("k_lo", [P, 2, S], F32R, c_mem)
            v_hi = sb("v_hi", [P, TB, W], F32R, c_mem)
            v_lo = sb("v_lo", [P, TB, W], F32R, c_mem)
            prob = sb("prob", [P, 2, PACKED], F32, c_mem)
            pt_hi = sb("pt_hi", [P, PACKED], F32R, c_mem)
            pt_lo = sb("pt_lo", [P, PACKED], F32R, c_mem)
        m_hi = sb("m_hi", [P, KB, S], F32R)
        m_lo = sb("m_lo", [P, KB, S], F32R)
        ln_g = t_a[:].rearrange("p a s -> p (a s)")
        ln_b = t_b[:].rearrange("p a s -> p (a s)")

        raw_in = [sem("raw_in0"), sem("raw_in1")]
        hi_rdy = [sem("hi_rdy0"), sem("hi_rdy1")]
        lo_rdy = [sem("lo_rdy0"), sem("lo_rdy1")]
        tile_done = [sem("tile_done0"), sem("tile_done1")]
        drained = [sem("drained0"), sem("drained1")]
        rows_in, wf_in, bf_in, x_in = sem("rows_in"), sem("wf_in"), sem("bf_in"), [sem("x_in0"), sem("x_in1")]
        sw_in, bs_in, lng_in, lnb_in, cn_in = sem("sw_in"), sem("bs_in"), sem("lng_in"), sem("lnb_in"), sem("cn_in")
        c_out, y_out = sem("c_out"), sem("y_out")
        const_rdy = sem("const_rdy")
        par_mm, par_rdy = sem("par_mm"), sem("par_rdy")
        x_mm, x_copied = sem("x_mm"), sem("x_copied")
        h_hi_rdy, h_rdy = sem("h_hi_rdy"), sem("h_rdy")
        sq_rdy, ssq_rdy = sem("sq_rdy"), sem("ssq_rdy")
        rms_mm, rms_sqrt, rms_rdy = sem("rms_mm"), sem("rms_sqrt"), sem("rms_rdy")
        silu_rdy, up_prod, act_hi_rdy, act_rdy = sem("silu_rdy"), sem("up_prod"), sem("act_hi_rdy"), sem("act_rdy")
        f_rows, f_turned = sem("f_rows"), sem("f_turned")
        wf_rdy, f_mm, f_steps, f_exp, f_ln, f_rdy = (
            sem("wf_rdy"), sem("f_mm"), sem("f_steps"), sem("f_exp"), sem("f_ln"), sem("f_rdy"))
        f_chain = sem("f_chain")
        c_mm, c_copied = sem("c_mm"), sem("c_copied")
        z_pad, z_rdy, conv0, conv1, conv2 = sem("z_pad"), sem("z_rdy"), sem("conv0"), sem("conv1"), sem("conv2")
        br_prod, br_hi_rdy, br_rdy = sem("br_prod"), sem("br_hi_rdy"), sem("br_rdy")
        gate_rdy = sem("gate_rdy")
        mg_add, m_hi_rdy, m_rdy = sem("mg_add"), sem("m_hi_rdy"), sem("m_rdy")
        sw_masked, sw_mm, sw_hi_rdy, sw_rdy = sem("sw_masked"), sem("sw_mm"), sem("sw_hi_rdy"), sem("sw_rdy")
        ln_stats, ln_mv, ln_sqrt, ln_rstd, ln_norm = (
            sem("ln_stats"), sem("ln_mv"), sem("ln_sqrt"), sem("ln_rstd"), sem("ln_norm"))
        ln_gained, vn_rdy = sem("ln_gained"), sem("vn_rdy")
        gelu_rdy, vn_hi_rdy, vns_rdy, sp_mm, sp_added = (
            sem("gelu_rdy"), sem("vn_hi_rdy"), sem("vns_rdy"), sem("sp_mm"), sem("sp_added"))
        qk_sq, qk_sqrt, qk_inv, qk_scale, qk_mm = (
            sem("qk_sq"), sem("qk_sqrt"), sem("qk_inv"), sem("qk_scale"), sem("qk_mm"))
        q_hi_rdy, k_hi_rdy = sem("q_hi_rdy"), sem("k_hi_rdy")
        v_hi_rdy = sem("v_hi_rdy")
        s_mm, s_taken, s_max, s_exp, s_rcp, p_rdy = (
            sem("s_mm"), sem("s_taken"), sem("s_max"), sem("s_exp"), sem("s_rcp"), sem("p_rdy"))
        pt_mm, pt_hi_rdy, pt_rdy, pv_mm, pv_hi_rdy, pv_taken = (
            sem("pt_mm"), sem("pt_hi_rdy"), sem("pt_rdy"), sem("pv_mm"), sem("pv_hi_rdy"), sem("pv_taken"))
        y_mm, y_copied = sem("y_mm"), sem("y_copied")

        FROM = 1

        block = ctx.enter_context(nc.Block())

        def over_pair(ap):
            return ap.unsqueeze(1).broadcast_to([P, 2, S])

        def pair(p):
            return ps[:, 2 * p:2 * p + 2, :]

        @block.sync
        def _(sp):
            sp.sem_inc(c_out, 16 * FROM)

            def load(dst, src, done):
                sp.dma_start(dst, src).then_inc(done, 16)

            def wide(s, T, w, l, c0):
                sp.wait_ge(lo_rdy[s], FROM + T)
                load(raw[:, s, :].rearrange("p (k n) -> p k n", n=W),
                     w[ds(l, 1), :, ds(c0, W)].rearrange("l (k p) n -> p (l k) n", p=P), raw_in[s])

            def tall(s, T, w, l, d):
                sp.wait_ge(lo_rdy[s], FROM + T)
                load(raw[:, s, 0:HK * P].rearrange("p (k n) -> p k n", n=P),
                     w[ds(l, 1), s * HK * P:(s + 1) * HK * P, ds(d * P, P)].rearrange(
                         "l (k p) n -> p (l k) n", p=P), raw_in[s])

            def param_rows(r, vec, l):
                v = vec[ds(l, 1)]
                v = v.rearrange("l (j p) -> (l j) p", p=P) if len(vec.shape) == 2 else \
                    v.rearrange("l w (j p) -> (l w j) p", p=P) if vec.shape[-1] > P else \
                    v.rearrange("l h p -> (l h) p")
                load(rows[r:r + v.shape[0], :], v, rows_in)

            for c in range(2):
                load(x_io[:, :, c * S:(c + 1) * S],
                     x[0][:, c * S:(c + 1) * S].rearrange("(t p) d -> p t d", p=P), x_in[c])
                if c == 0:
                    param_rows(0, ffn1_norm, 0)

            def ffn(l, w_gu, w_down, t_up, t_dn, between=None):
                with sp.Fori(0, NU) as i:
                    wide(0, l * T_ALL + t_up + i, w_gu, l, i * W)
                    wide(1, l * T_ALL + t_up + i, w_gu, l, FF + i * W)
                if between:
                    between(l)
                with sp.Fori(0, KB) as d:
                    tall(0, l * T_ALL + t_dn + d, w_down, l, d)
                    tall(1, l * T_ALL + t_dn + d, w_down, l, d)

            def square_matrix(l, w, t0):
                with sp.Fori(0, 2) as i:
                    for s in range(2):
                        wide(s, l * T_ALL + t0 + i, w, l, (2 * i + s) * W)

            def small_parameters(l):
                sp.wait_ge(par_mm, l + 1)
                param_rows(R_MIX, mix_norm, l)
                param_rows(R_CONV, conv_w, l)
                param_rows(R_GATE, b_gate, l)
                param_rows(R_Q, q_norm_g, l)
                param_rows(R_K, k_norm_g, l)
                param_rows(R_FFN2, ffn2_norm, l)
                param_rows(R_NEXT, ffn1_norm, (l + 1) % L)
                sp.wait_ge(wf_rdy, FROM + l)
                load(wf_raw[:], w_in[ds(l, 1), :, C_F:C_F + H].rearrange("l (k p) n -> p (l k) n", p=P), wf_in)
                sp.wait_ge(f_steps, FROM + 2 * l)
                load(bf_bc[:], b_forget[ds(l, 1)].rearrange("l h -> (l h)").partition_broadcast(P), bf_in)

            with sp.Fori(0, L) as l:
                ffn(l, ffn1_w_gu, ffn1_w_down, T_UP1, T_DN1, small_parameters)
                with sp.Fori(0, NJ) as i:
                    T = l * T_ALL + T_A + 2 * i
                    wide(0, T, w_in, l, C_C + i * W)
                    wide(1, T, w_in, l, C_X + i * W)
                    wide(0, T + 1, w_in, l, C_B + i * W)
                    wide(1, T + 1, w_in, l, C_G + i * W)
                sp.wait_ge(tile_done[1], l * T_ALL + T_A)
                load(sw_raw[:], sgu_w[ds(l, 1)].rearrange("l g t s -> t (l g) s"), sw_in)
                load(bs_bc[:], sgu_b[ds(l, 1)].rearrange("l g t -> (l g) t").partition_broadcast(P), bs_in)
                with sp.Fori(0, 2) as i:
                    for s in range(2):
                        wide(s, l * T_ALL + T_BV + i, w_in, l, C_SV + (2 * i + s) * W)
                sp.wait_ge(gate_rdy, FROM + (3 * l + 1) * NJ)
                load(ln_g, sgu_ln_g[ds(l, 1)].rearrange("l d -> (l d)").partition_broadcast(P), lng_in)
                load(ln_b, sgu_ln_b[ds(l, 1)].rearrange("l d -> (l d)").partition_broadcast(P), lnb_in)
                square_matrix(l, w_out_conv, T_WA)
                sp.wait_ge(c_copied, 2 * l + 2)
                sp.dma_start(c_dram, c_neg[:]).then_inc(c_out, 16)
                with sp.Fori(0, NJ) as i:
                    wide(0, l * T_ALL + T_BU + i, w_in, l, C_SU + i * W)
                    wide(1, l * T_ALL + T_BU + i, w_in, l, C_G + D + i * W)
                square_matrix(l, w_out_sgu, T_WB)
                with sp.Fori(0, NJ) as i:
                    T = l * T_ALL + T_C + 2 * i
                    wide(0, T, w_in, l, C_Q + i * W)
                    wide(1, T, w_in, l, C_K + i * W)
                    wide(0, T + 1, w_in, l, C_V + i * W)
                    wide(1, T + 1, w_in, l, C_G + 2 * D + i * W)
                    sp.wait_ge(c_out, 16 * FROM + 16 * (l + 1))
                    sp.wait_ge(s_taken, FROM + l * H + 2 * i)
                    load(cn_bc[:], c_dram[ds(2 * i, 2), :].partition_broadcast(P), cn_in)
                square_matrix(l, w_out_attn, T_WC)
                square_matrix(l, w_o, T_WO)
                ffn(l, ffn2_w_gu, ffn2_w_down, T_UP2, T_DN2)
            wide(0, L * T_ALL, ffn1_w_gu, 0, 0)
            wide(1, L * T_ALL, ffn1_w_gu, 0, FF)
            for t in range(TB):
                sp.wait_ge(y_copied, t + 1)
                sp.dma_start(out[0, t * P:(t + 1) * P, :], x_io[:, t, :]).then_inc(y_out, 16)
            sp.wait_ge(y_out, 16 * TB)

        @block.tensor
        def _(pe):
            for counted in (sp_mm, s_mm, pv_mm, f_mm):
                pe.sem_inc(counted, FROM)

            def mm(o, lhs, rhs, start, stop, **kw):
                return nc.tensor.matmul(o, lhs, rhs, start=start, stop=stop, **kw)

            def split_mm(o, terms):
                last = len(terms) - 1
                for n, ((ah, al), (bh, bl)) in enumerate(terms):
                    mm(o, ah, bh, n == 0, False)
                    mm(o, ah, bl, False, False)
                    done = mm(o, al, bh, False, n == last)
                return done

            def w_block(s, k, c, n=W):
                at = k * n + c * P
                return w_hi[:, s, at:at + P], w_lo[:, s, at:at + P]

            def take(s, T, p, U):
                pe.wait_ge(lo_rdy[s], FROM + T + 1)
                pe.wait_ge(drained[p], FROM + U)

            def wide_part(s, r_hi, r_lo, ks, cs=(0, 1)):
                for c in cs:
                    for k in ks:
                        wh, wl = w_block(s, k, c)
                        o = ps[:, 2 * s + c, :]
                        mm(o, wh, r_hi[:, k, :], k == 0, False)
                        mm(o, wh, r_lo[:, k, :], False, False)
                        done = mm(o, wl, r_hi[:, k, :], False, k == KB - 1)
                return done

            def wide(s, T, U, r_hi, r_lo, rdy=None, value=None, last=1):
                take(s, T, s, U)
                if rdy is None:
                    wide_part(s, r_hi, r_lo, range(KB)).then_inc(tile_done[s], 1)
                else:
                    pe.wait_ge(rdy, value - last)
                    wide_part(s, r_hi, r_lo, range(KB - 2))
                    pe.wait_ge(rdy, value)
                    wide_part(s, r_hi, r_lo, range(KB - 2, KB)).then_inc(tile_done[s], 1)

            def first_wide(T, U, norm):
                take(0, T, 0, U)
                for k in range(KB):
                    pe.wait_ge(h_rdy, KB * norm + k + 1)
                    done = wide_part(0, h_hi, h_lo, (k,))
                done.then_inc(tile_done[0], 1)

            def tok_part(s, t):
                tok = slice(t * P, (t + 1) * P)
                return split_mm(ps[:, 2 * s + t // 2, (t % 2) * W:(t % 2 + 1) * W],
                                [((h_hi[:, k, tok], h_lo[:, k, tok]),
                                  (w_hi[:, s, k * W:(k + 1) * W], w_lo[:, s, k * W:(k + 1) * W]))
                                 for k in range(KB)])

            def wide_tok(s, T, U, between=None):
                take(s, T, s, U)
                for t in range(TB):
                    if t == TB - 1 and between:
                        between()
                    done = tok_part(s, t)
                done.then_inc(tile_done[s], 1)

            def turn(o, src, n=P):
                return nc.tensor.transpose(o, src, ident[0:n, 0:n])

            def rms_sums(n):
                pe.wait_ge(ssq_rdy, KB * (n + 1))
                pe.wait_ge(rms_sqrt, FROM + n)
                mm(ps[:, 4, :], ones[:], sq[:, 1, :], True, True)
                for t in range(TB):
                    done = mm(ps[:, 5, t:t + 1], sq[:, 1, t * P:(t + 1) * P], ones[:, 0:1], True, True)
                done.then_inc(rms_mm, 1)

            pe.wait_ge(const_rdy, CONSTS)
            pe.wait_ge(rows_in, 16)
            turn(ps[:, 7, 0:KB], rows[0:KB, :], KB).then_inc(par_mm, 1)
            for d in range(KB):
                if d % (KB // 2) == 0:
                    pe.wait_ge(x_in[2 * d // KB], 16)
                if d == KB - 1:
                    pe.wait_ge(par_rdy, 1)
                for t in range(TB):
                    done = turn(ps[:, d, t * P:(t + 1) * P], x_io[:, t, d * P:(d + 1) * P])
                done.then_inc(x_mm, 1)
            def ffn(l, f, t_up, u_up, t_dn, u_dn, norm, between=None):
                first_wide(l * T_ALL + t_up, l * U_ALL + u_up, norm)
                rms_sums(norm)
                wide(1, l * T_ALL + t_up, l * U_ALL + u_up, h_hi, h_lo)
                with pe.Fori(1, NU) as i:
                    for s in range(2):
                        wide(s, l * T_ALL + t_up + i, l * U_ALL + u_up + i, h_hi, h_lo)
                if between:
                    between(l)
                with pe.Fori(0, KB // 2) as i:
                    for e in range(2):
                        T = l * T_ALL + t_dn + 2 * i + e
                        for s in range(2):
                            take(s, T, e, l * U_ALL + u_dn + i)
                            pe.wait_ge(act_rdy, FROM + NU * (2 * l + f) + ((HK + 1) // 2, NU - 1)[s])
                            for k in range(HK):
                                if s == 1 and k == HK - 2:
                                    pe.wait_ge(act_rdy, FROM + NU * (2 * l + f + 1))
                                lh, ll = w_block(s, k, 0, P)
                                f_ = s * HK + k
                                o = ps[:, 2 * e, :]
                                mm(o, lh, act_hi[:, f_, :], f_ == 0, False)
                                mm(o, lh, act_lo[:, f_, :], False, False)
                                done = mm(o, ll, act_hi[:, f_, :], False, f_ == FB - 1)
                            done.then_inc(tile_done[s], 1)

            def square_matrix(l, t0, u0, r_hi, r_lo, rdy, value):
                with pe.Fori(0, 2) as i:
                    for s in range(2):
                        wide(s, l * T_ALL + t0 + i, l * U_ALL + u0 + i, r_hi, r_lo, rdy, value)

            def scores(l, i, b):
                n = l * H + 2 * i + b
                for s in range(2):
                    pe.wait_ge(drained[s], FROM + l * U_ALL + U_C + 3 * i + 2)
                pe.wait_ge(s_taken, FROM + n)
                pe.wait_ge(pt_rdy, FROM + n - b if b else n)
                for t in range(TB):
                    tok, keys = slice(t * P, (t + 1) * P), (t + 1) * P
                    o = packed[:, Q_OFF[t]:Q_OFF[t] + keys]
                    mm(o, q_hi[:, b, tok], k_hi[:, b, 0:keys], True, False)
                    mm(o, q_hi[:, b, tok], k_lo[:, b, 0:keys], False, False)
                    mm(o, q_lo[:, b, tok], k_hi[:, b, 0:keys], False, False)
                    done = mm(o[:, keys - P:keys], ident_b[:], causal_b[:], False, True)
                done.then_inc(s_mm, 1)

            def turn_probs(l, i, b):
                n = l * H + 2 * i + b
                pe.wait_ge(p_rdy, n + 1)
                pe.wait_ge(s_taken, FROM + l * H + 2 * i + 2)
                pe.wait_ge(pt_rdy, FROM + n)
                for t in range(TB):
                    for k in range(t + 1):
                        at = K_OFF[k] + (t - k) * P
                        done = turn(packed[:, at:at + P], prob[:, b, Q_OFF[t] + k * P:Q_OFF[t] + (k + 1) * P])
                done.then_inc(pt_mm, 1)

            def weigh_values(l, i, b):
                n = l * H + 2 * i + b
                pe.wait_ge(pt_rdy, FROM + n + 1)
                pe.wait_ge(pv_taken, FROM + n)
                for k in range(TB):
                    o = ps[:, 7, k * P:S]
                    cols, at = slice(b * P, (b + 1) * P), slice(K_OFF[k], K_OFF[k] + S - k * P)
                    mm(o, v_hi[:, k, cols], pt_hi[:, at], k == 0, False)
                    mm(o, v_hi[:, k, cols], pt_lo[:, at], False, False)
                    done = mm(o, v_lo[:, k, cols], pt_hi[:, at], False, k == TB - 1)
                done.then_inc(pv_mm, 1)

            def turn_heads(n, p, U, src):
                pe.wait_ge(drained[p], FROM + U)
                for b in range(2):
                    for t in range(TB):
                        at = t * W + b * P
                        done = turn(ps[:, 2 * p + b, t * P:(t + 1) * P],
                                    src[:].rearrange("p a s -> p (a s)")[:, at:at + P])
                done.then_inc(qk_mm, 1)

            def attention_pair(l, i, prev):
                T, U = l * T_ALL + T_C + 2 * i, l * U_ALL + U_C + 3 * i
                n = 2 * (l * NJ + i)
                wide_tok(0, T, U)
                if prev:
                    scores(l, i - 1, 1)
                wide_tok(1, T, U, lambda: turn_heads(n, 0, U + 1, t_a))
                if prev:
                    turn_probs(l, i - 1, 0)
                wide_tok(0, T + 1, U + 2, lambda: turn_heads(n + 1, 1, U + 1, t_b))
                if prev:
                    weigh_values(l, i - 1, 0)
                    turn_probs(l, i - 1, 1)
                take(1, T + 1, 1, U + 2)
                wide_part(1, h_hi, h_lo, range(KB), (0,))
                if prev:
                    weigh_values(l, i - 1, 1)
                wide_part(1, h_hi, h_lo, range(KB), (1,)).then_inc(tile_done[1], 1)
                scores(l, i, 0)

            def turn_parameters(l):
                pe.wait_ge(rows_in, 16 * (7 * l + 8))
                pe.wait_ge(par_rdy, l + 1)
                pe.wait_ge(pv_taken, FROM + l * H)
                turn(ps[:, 7, 0:ROWS], rows[0:ROWS, :], ROWS).then_inc(par_mm, 1)

            with pe.Fori(0, L) as l:
                ffn(l, 0, T_UP1, U_UP1, T_DN1, U_DN1, 3 * l, turn_parameters)

                T, U = l * T_ALL + T_A, l * U_ALL + U_A
                first_wide(T, U, 3 * l + 1)
                rms_sums(3 * l + 1)
                pe.wait_ge(wf_rdy, FROM + l + 1)
                for k in range(KB):
                    done = mm(ps[0:H, 6, :], wf[:, k, :], xT[:, k, :], k == 0, k == KB - 1)
                done.then_inc(f_mm, 1)
                take(1, T, 1, U)
                wide_part(1, h_hi, h_lo, range(KB - 1))
                pe.wait_ge(f_rows, l + 1)
                pe.wait_ge(par_rdy, l + 2)
                wide_part(1, h_hi, h_lo, (KB - 1,)).then_inc(tile_done[1], 1)
                for t in range(TB):
                    done = turn(ps[:, 7, t * H:(t + 1) * H], c_neg[:, t * P:(t + 1) * P], H)
                done.then_inc(f_turned, 1)
                for s in (0, 1):
                    wide(s, T + 1, U + 1, h_hi, h_lo)
                with pe.Fori(1, NJ) as i:
                    for s in (0, 1):
                        wide(s, l * T_ALL + T_A + 2 * i, l * U_ALL + U_A + 2 * i, h_hi, h_lo)
                    for s in (0, 1):
                        wide(s, l * T_ALL + T_A + 2 * i + 1, l * U_ALL + U_A + 2 * i + 1, h_hi, h_lo)
                pe.wait_ge(sw_masked, l + 1)
                pe.wait_ge(rms_sqrt, FROM + 3 * l + 2)
                for g in range(H):
                    done = turn(ps[:, 4 + g // 4, (g % 4) * P:(g % 4 + 1) * P], sw_raw[:, g, :])
                done.then_inc(sw_mm, 1)
                with pe.Fori(0, 2) as i:
                    for s in range(2):
                        wide_tok(s, l * T_ALL + T_BV + i, l * U_ALL + U_BV + i)
                pe.wait_ge(f_rdy, l + 1)
                for t in range(TB):
                    for j in range(t + 1):
                        m = upper if j == t else ones
                        mm(ps[:, 6, t * H:(t + 1) * H], m[:], lf[:, 0, j, :], j == 0, j == t)
                        done = mm(ps[0:H, 7, t * P:(t + 1) * P], lf[:, 0, j, :], m[:], j == 0, j == t)
                done.then_inc(c_mm, 1)
                square_matrix(l, T_WA, U_WA, br_hi, br_lo, br_rdy, FROM + (2 * l + 1) * NJ)
                with pe.Fori(0, NJ) as i:
                    for s in range(2):
                        wide(s, l * T_ALL + T_BU + i, l * U_ALL + U_BU + i, h_hi, h_lo)
                    pe.wait_ge(sw_rdy, l + 1)
                    pe.wait_ge(vns_rdy, l * NJ + i + 1)
                    pe.wait_ge(sp_added, FROM + l * NJ + i)
                    for b in range(2):
                        for t in range(TB):
                            cols = slice(b * P, (b + 1) * P)
                            wh = sw_hi[:, ds(2 * i + b, 1), :].rearrange("p g t -> p (g t)")
                            wl = sw_lo[:, ds(2 * i + b, 1), :].rearrange("p g t -> p (g t)")
                            done = split_mm(ps[:, 4 + b, t * P:(t + 1) * P],
                                            [((vn_hi[:, t, cols], vn_lo[:, t, cols]), (wh, wl))])
                    done.then_inc(sp_mm, 1)
                square_matrix(l, T_WB, U_WB, br_hi, br_lo, br_rdy, FROM + (2 * l + 2) * NJ)

                pe.wait_ge(sp_added, FROM + (l + 1) * NJ)
                pe.wait_ge(c_copied, 2 * l + 2)
                attention_pair(l, 0, False)
                with pe.Fori(1, NJ) as i:
                    attention_pair(l, i, True)
                T, U = l * T_ALL + T_WC, l * U_ALL + U_WC

                def out_part(s, ks, cs=(0, 1)):
                    return wide_part(s, br_hi, br_lo, ks, cs)

                take(0, T, 0, U)
                pe.wait_ge(pv_taken, FROM + (l + 1) * H - 2)
                out_part(0, range(H - 2), (0,))
                scores(l, NJ - 1, 1)
                out_part(0, range(H - 2), (1,))
                take(1, T, 1, U)
                out_part(1, (0,), (0,))
                turn_probs(l, NJ - 1, 0)
                out_part(1, range(1, H - 2), (0,))
                weigh_values(l, NJ - 1, 0)
                turn_probs(l, NJ - 1, 1)
                out_part(1, (0, 1), (1,))
                pe.wait_ge(pv_taken, FROM + (l + 1) * H - 1)
                out_part(0, (H - 2,))
                out_part(1, (H - 2,), (0,))
                weigh_values(l, NJ - 1, 1)
                out_part(1, (2, 3), (1,))
                pe.wait_ge(pv_taken, FROM + (l + 1) * H)
                out_part(0, (H - 1,)).then_inc(tile_done[0], 1)
                out_part(1, (H - 1,), (0,))
                out_part(1, range(4, H), (1,)).then_inc(tile_done[1], 1)
                for s in range(2):
                    wide(s, T + 1, U + 1, br_hi, br_lo)
                square_matrix(l, T_WO, U_WO, m_hi, m_lo, m_rdy, FROM + (l + 1) * NJ)
                ffn(l, 1, T_UP2, U_UP2, T_DN2, U_DN2, 3 * l + 2)

            for s in range(2):
                pe.wait_ge(drained[s], FROM + L * U_ALL)
            for t in range(TB):
                for d in range(KB):
                    done = turn(ps[:, 2 * t + d // 4, (d % 4) * P:(d % 4 + 1) * P], xT[:, d, t * P:(t + 1) * P])
                done.then_inc(y_mm, 1)

        @block.scalar
        def _(act):
            for counted in (gate_rdy, rms_sqrt):
                act.sem_inc(counted, FROM)

            def copy(o, a, scale=1.0):
                return nc.scalar.activation(o, a, ACT.Copy, scale=scale)

            def split_hi(s, T):
                act.wait_ge(raw_in[s], 16 * (T + 1))
                act.wait_ge(tile_done[s], T)
                copy(w_hi[:, s, :], raw[:, s, :]).then_inc(hi_rdy[s], 1)

            def h_blocks(d, n, r):
                for b in range(n):
                    copy(h_hi[:, ds(d + b, 1), :], xT[:, ds(d + b, 1), :], par[:, ds(r + d + b, 1)]).then_inc(h_hi_rdy, 1)

            def rms_roots(n):
                act.wait_ge(rms_mm, n + 1)
                nc.scalar.activation(rinv[:], ps[:, 4, :], ACT.Sqrt, bias=eps_rms[:], scale=1.0 / D)
                nc.scalar.activation(rtok[:], ps[:, 5, 0:TB], ACT.Sqrt, bias=eps_rms[:],
                                     scale=1.0 / D).then_inc(rms_sqrt, 1)

            def gates(i, br):
                for b in range(2):
                    done = nc.scalar.activation(gate[:, ds(2 * i + b, 1), :], t_b[:, b:b + 1, :], ACT.Sigmoid,
                                                bias=par[:, ds(R_GATE + br * KB + 2 * i + b, 1)])
                done.then_inc(gate_rdy, 1)

            def branch_hi(n, i):
                act.wait_ge(br_prod, n + 1)
                copy(br_hi[:, ds(2 * i, 2), :], t_a[:]).then_inc(br_hi_rdy, 1)

            act.wait_ge(const_rdy, CONSTS)
            act.wait_ge(par_rdy, 1)
            for first, end in ((0, 2), (2, KB)):
                with act.Fori(first, end) as d:
                    act.wait_ge(x_copied, d + 1)
                    h_blocks(d, 1, R_NEXT)
                split_hi(first // 2, 0)

            def ffn(l, f, t_up, u_up, t_dn, u_dn, norm, r, between=None):
                rms_roots(norm)
                with act.Fori(0, NU) as i:
                    T, U, n = l * T_ALL + t_up + i, l * U_ALL + u_up + i, (2 * l + f) * NU + i
                    split_hi(0, T + 1)
                    act.wait_ge(drained[0], FROM + U + 1)
                    nc.scalar.activation(t_a[:], t_a[:], ACT.Silu).then_inc(silu_rdy, 1)
                    split_hi(1, T + 1)
                    act.wait_ge(up_prod, n + 1)
                    copy(act_hi[:, ds(2 * i, 2), :], t_b[:]).then_inc(act_hi_rdy, 1)
                if between:
                    between(l)
                with act.Fori(0, KB // 2) as i:
                    for e in range(2):
                        T, U = l * T_ALL + t_dn + 2 * i + e, l * U_ALL + u_dn + i
                        split_hi(0, T + 1)
                        act.wait_ge(drained[e], FROM + U + 1)
                        h_blocks(2 * i + e, 1, r)
                        split_hi(1, T + 1)

            def plain_tiles(l, t0, count=2):
                with act.Fori(0, count) as i:
                    for s in range(2):
                        split_hi(s, l * T_ALL + t0 + i + 1)

            def exps(l, i, b):
                n = l * H + 2 * i + b
                act.wait_ge(s_max, n + 1)
                for t in range(TB):
                    cols = slice(Q_OFF[t], Q_OFF[t] + (t + 1) * P)
                    done = nc.scalar.activation(prob[:, b, cols], prob[:, b, cols], ACT.Exp,
                                                bias=nmax[:, b, t:t + 1], accum_out=esum[:, b, t:t + 1])
                done.then_inc(s_exp, 1)

            def probs_hi(l, i, b):
                n = l * H + 2 * i + b
                act.wait_ge(pt_mm, n + 1)
                act.wait_ge(pv_mm, FROM + n)
                copy(pt_hi[:], packed).then_inc(pt_hi_rdy, 1)

            def heads_hi(l, i, b):
                n = l * H + 2 * i + b
                act.wait_ge(pv_mm, FROM + n + 1)
                copy(br_hi[:, ds(2 * i + b, 1), :], ps[:, 7:8, :]).then_inc(pv_hi_rdy, 1)

            def head_roots(p, T, dst, n):
                act.wait_ge(tile_done[p], T + 1)
                for t in range(TB):
                    for b in range(2):
                        g = 2 * t + b
                        done = nc.scalar.activation(dst[:, t // 2, (g % 4) * P:(g % 4 + 1) * P],
                                             ps[:, 2 * p + t // 2, (g % 4) * P:(g % 4 + 1) * P], ACT.Square,
                                             scale=rtok[:, t:t + 1], accum_out=hsum[:, g:g + 1])
                done.then_inc(qk_sq, 1)
                act.wait_ge(qk_sq, n + 1)
                nc.scalar.activation(hsum[:], hsum[:], ACT.Sqrt, bias=eps_rms[:], scale=1.0 / P).then_inc(qk_sqrt, 1)

            def gained_hi(o_hi, p, r, i, n, rdy):
                act.wait_ge(qk_mm, n + 1)
                for b in range(2):
                    done = copy(o_hi[:, b:b + 1, :], ps[:, 2 * p + b:2 * p + b + 1, :], par[:, ds(r + 2 * i + b, 1)])
                done.then_inc(rdy, 1)

            def attention_pair(l, i, prev):
                T, U = l * T_ALL + T_C + 2 * i, l * U_ALL + U_C + 3 * i
                n = l * NJ + i
                if prev:
                    exps(l, i - 1, 0)
                act.wait_ge(mg_add, FROM + 8 * l + 4)
                act.wait_ge(gate_rdy, FROM + (3 * l + 2) * NJ + i)
                head_roots(0, T, t_a, 2 * n)
                split_hi(0, T + 1)
                act.wait_ge(s_mm, FROM + l * H + 2 * i)
                gained_hi(q_hi, 0, R_Q, i, 2 * n, q_hi_rdy)
                if prev:
                    exps(l, i - 1, 1)
                head_roots(1, T, t_b, 2 * n + 1)
                split_hi(1, T + 1)
                if prev:
                    probs_hi(l, i - 1, 0)
                gained_hi(k_hi, 1, R_K, i, 2 * n + 1, k_hi_rdy)
                if prev:
                    heads_hi(l, i - 1, 0)
                    probs_hi(l, i - 1, 1)
                split_hi(0, T + 2)
                if prev:
                    heads_hi(l, i - 1, 1)
                for t in range(TB):
                    done = copy(v_hi[:, t, :], ps[:, t // 2, (t % 2) * W:(t % 2 + 1) * W], rtok[:, t:t + 1])
                done.then_inc(v_hi_rdy, 1)
                split_hi(1, T + 2)
                act.wait_ge(drained[1], FROM + U + 3)
                gates(i, 2)

            with act.Fori(0, L) as l:
                ffn(l, 0, T_UP1, U_UP1, T_DN1, U_DN1, 3 * l, R_MIX)
                rms_roots(3 * l + 1)

                with act.Fori(0, NJ) as i:
                    T, U, n = l * T_ALL + T_A + 2 * i, l * U_ALL + U_A + 2 * i, l * NJ + i
                    split_hi(0, T + 1)
                    split_hi(1, T + 1)
                    act.wait_ge(z_rdy, n + 1)
                    for b in range(2):
                        done = copy(y_c[:, b:b + 1, :], z[:, b:b + 1, 2:S + 2], par[:, ds(R_CONV + 2 * KB + 2 * i + b, 1)])
                    done.then_inc(conv0, 1)
                    split_hi(0, T + 2)
                    branch_hi(2 * l * NJ + i, i)
                    split_hi(1, T + 2)
                    act.wait_ge(drained[1], FROM + U + 2)
                    gates(i, 0)
                act.wait_ge(f_steps, FROM + 2 * l + 1)
                nc.scalar.activation(lf[:, 2], lf[:, 1], ACT.Exp).then_inc(f_exp, 1)
                act.wait_ge(f_steps, FROM + 2 * l + 2)
                nc.scalar.activation(lf[:, 4], lf[:, 3], ACT.Ln).then_inc(f_ln, 1)
                act.wait_ge(sw_mm, l + 1)
                copy(sw_hi[:], ps[:, 4:6, :].rearrange("p a (g t) -> p (a g) t", t=P)).then_inc(sw_hi_rdy, 1)
                act.wait_ge(rms_rdy, 3 * l + 2)
                with act.Fori(0, 2) as i:
                    for s in range(2):
                        T = l * T_ALL + T_BV + i
                        split_hi(s, T + 1)
                        for t in range(TB):
                            done = nc.scalar.activation(
                                vn[:, t, ds((2 * i + s) * W, W)], ps[:, 2 * s + t // 2, (t % 2) * W:(t % 2 + 1) * W],
                                ACT.Gelu, scale=rtok[:, t:t + 1])
                        done.then_inc(drained[s], 1)
                act.wait_ge(ln_mv, l + 1)
                nc.scalar.activation(rstd[:], mv[:, :, 1], ACT.Sqrt, bias=eps_ln[:]).then_inc(ln_sqrt, 1)
                plain_tiles(l, T_WA)
                with act.Fori(0, NJ) as i:
                    T, U, n = l * T_ALL + T_BU + i, l * U_ALL + U_BU + i, l * NJ + i
                    split_hi(0, T + 1)
                    act.wait_ge(drained[0], FROM + U + 1)
                    nc.scalar.activation(t_a[:], t_a[:], ACT.Gelu).then_inc(gelu_rdy, 1)
                    act.wait_ge(vn_rdy, TB * (l + 1))
                    act.wait_ge(sp_mm, FROM + n)
                    copy(vn_hi[:], vn[:, :, ds(i * W, W)]).then_inc(vn_hi_rdy, 1)
                    split_hi(1, T + 1)
                    act.wait_ge(drained[1], FROM + U + 1)
                    gates(i, 1)
                    branch_hi((2 * l + 1) * NJ + i, i)
                plain_tiles(l, T_WB)
                attention_pair(l, 0, False)
                with act.Fori(1, NJ) as i:
                    attention_pair(l, i, True)
                for b in range(2):
                    exps(l, NJ - 1, b)
                for b in range(2):
                    probs_hi(l, NJ - 1, b)
                    heads_hi(l, NJ - 1, b)
                with act.Fori(0, 2) as i:
                    for s in range(2):
                        split_hi(s, l * T_ALL + T_WC + i + 1)
                        act.wait_ge(mg_add, FROM + 8 * l + 4 + 2 * i + s + 1)
                        copy(m_hi[:, ds(4 * i + 2 * s, 2), :], (t_a, t_b)[s][:]).then_inc(m_hi_rdy, 1)
                with act.Fori(0, 2) as i:
                    for s in range(2):
                        split_hi(s, l * T_ALL + T_WO + i + 1)
                        act.wait_ge(drained[s], FROM + l * U_ALL + U_WO + i + 1)
                        h_blocks(4 * i + 2 * s, 2, R_FFN2)
                ffn(l, 1, T_UP2, U_UP2, T_DN2, U_DN2, 3 * l + 2, R_NEXT)
            for t in (1, 3):
                act.wait_ge(y_mm, t + 1)
                act.wait_ge(y_copied, t)
                copy(x_io[:, t, :], ps[:, 2 * t:2 * t + 2, :].rearrange("p a s -> p (a s)")).then_inc(y_copied, 1)

        @block.vector
        def _(dve):
            V = nc.vector
            for counted in (*lo_rdy, *drained, wf_rdy, f_steps, s_taken, br_rdy, sp_added, pt_rdy, pv_taken,
                            m_rdy, mg_add, act_rdy):
                dve.sem_inc(counted, FROM)

            def split_lo(s, T):
                dve.wait_ge(hi_rdy[s], T + 1)
                V.tensor_tensor(w_lo[:, s, :], raw[:, s, :], w_hi[:, s, :].bitcast(F32), ALU.subtract).then_inc(lo_rdy[s], 1)

            def h_blocks(d, n, r, count):
                dve.wait_ge(h_hi_rdy, count)
                for b in range(n):
                    V.scalar_tensor_tensor(
                        out=h_lo[:, ds(d + b, 1), :], in0=xT[:, ds(d + b, 1), :], scalar=par[:, ds(r + d + b, 1)],
                        in1=h_hi[:, ds(d + b, 1), :].bitcast(F32), op0=ALU.mult,
                        op1=ALU.subtract).then_inc(h_rdy, 1)

            def rms_inverse(n):
                dve.wait_ge(rms_sqrt, FROM + n + 1)
                V.reciprocal(rinv[:], rinv[:])
                V.reciprocal(rtok[:], rtok[:]).then_inc(rms_rdy, 1)

            def take(p, T, U, dst):
                dve.wait_ge(tile_done[p], T + 1)
                V.tensor_tensor(dst[:], pair(p), over_pair(rinv[:]), ALU.mult).then_inc(drained[p], 1)

            def branch_lo(n, i):
                dve.wait_ge(br_hi_rdy, n + 1)
                V.tensor_tensor(br_lo[:, ds(2 * i, 2), :], t_a[:], br_hi[:, ds(2 * i, 2), :].bitcast(F32),
                                ALU.subtract).then_inc(br_rdy, 1)

            dve.wait_ge(par_mm, 1)
            V.tensor_copy(par[:, R_NEXT:R_NEXT + KB], ps[:, 7, 0:KB]).then_inc(par_rdy, 1)
            dve.wait_ge(x_mm, 1)
            V.tensor_copy(xT[:, 0, :], ps[:, 0, :]).then_inc(x_copied, 1)
            for first, end in ((1, 3), (3, KB)):
                with dve.Fori(first, end) as d:
                    dve.wait_ge(x_mm, d + 1)
                    V.tensor_copy(xT[:, ds(d, 1), :], ps[:, ds(d, 1), :]).then_inc(x_copied, 1)
                    h_blocks(d - 1, 1, R_NEXT, d)
                if end == KB:
                    h_blocks(KB - 1, 1, R_NEXT, KB)
                split_lo(first // 2, 0)

            def ffn(l, f, t_up, u_up, t_dn, u_dn, norm, r, between=None):
                rms_inverse(norm)
                with dve.Fori(0, NU) as i:
                    T, U, n = l * T_ALL + t_up + i, l * U_ALL + u_up + i, (2 * l + f) * NU + i
                    dve.wait_ge(rms_rdy, norm + 1)
                    take(0, T, U, t_a)
                    split_lo(0, T + 1)
                    dve.wait_ge(act_rdy, FROM + n)
                    take(1, T, U, t_b)
                    dve.wait_ge(silu_rdy, n + 1)
                    dve.wait_ge(drained[1], FROM + U + 1)
                    V.tensor_tensor(t_b[:], t_a[:], t_b[:], ALU.mult).then_inc(up_prod, 1)
                    split_lo(1, T + 1)
                    dve.wait_ge(act_hi_rdy, n + 1)
                    V.tensor_tensor(act_lo[:, ds(2 * i, 2), :], t_b[:], act_hi[:, ds(2 * i, 2), :].bitcast(F32),
                                    ALU.subtract).then_inc(act_rdy, 1)
                if between:
                    between(l)
                with dve.Fori(0, KB // 2) as i:
                    for e in range(2):
                        T, U, d = l * T_ALL + t_dn + 2 * i + e, l * U_ALL + u_dn + i, 2 * i + e
                        split_lo(0, T + 1)
                        dve.wait_ge(tile_done[1], T + 1)
                        V.scalar_tensor_tensor(out=xT[:, ds(d, 1), :], in0=ps[:, 2 * e:2 * e + 1, :], scalar=0.5,
                                               in1=xT[:, ds(d, 1), :], op0=ALU.mult, op1=ALU.add).then_inc(drained[e], 1)
                        dve.wait_ge(drained[e], FROM + U + 1)
                        h_blocks(d, 1, r, KB * (norm + 1) + d + 1)
                        split_lo(1, T + 1)

            def softmax_head(l, i, b):
                n = l * H + 2 * i + b
                dve.wait_ge(s_mm, FROM + n + 1)
                dve.wait_ge(cn_in, 16 * (l * NJ + i + 1))
                for t in range(TB):
                    keys = (t + 1) * P
                    cols = slice(Q_OFF[t], Q_OFF[t] + keys)
                    done = V.scalar_tensor_tensor(
                        out=prob[:, b, cols], in0=cn_bc[:, b, 0:keys],
                        scalar=c_tok[:, t, ds(2 * i + b, 1)], in1=packed[:, cols],
                        op0=ALU.add, op1=ALU.add)
                done.then_inc(s_taken, 1)
                dve.wait_ge(s_taken, FROM + n + 1)
                for t in range(TB):
                    done = V.tensor_reduce(nmax[:, b, t:t + 1], prob[:, b, Q_OFF[t]:Q_OFF[t] + (t + 1) * P],
                                           AX_X, ALU.max, negate=True)
                done.then_inc(s_max, 1)

            def softmax_scale(l, i, b):
                n = l * H + 2 * i + b
                dve.wait_ge(s_exp, n + 1)
                V.reciprocal(esum[:, b, :], esum[:, b, :]).then_inc(s_rcp, 1)
                dve.wait_ge(s_rcp, n + 1)
                for t in range(TB):
                    cols = slice(Q_OFF[t], Q_OFF[t] + (t + 1) * P)
                    done = V.tensor_scalar(prob[:, b, cols], prob[:, b, cols], esum[:, b, t:t + 1], None, ALU.mult)
                done.then_inc(p_rdy, 1)

            def probs_lo(l, i, b):
                n = l * H + 2 * i + b
                dve.wait_ge(pt_hi_rdy, n + 1)
                V.tensor_tensor(pt_lo[:], packed, pt_hi[:].bitcast(F32), ALU.subtract).then_inc(pt_rdy, 1)

            def heads_lo(l, i, b):
                n = l * H + 2 * i + b
                dve.wait_ge(pv_hi_rdy, n + 1)
                V.tensor_tensor(br_lo[:, ds(2 * i + b, 1), :], ps[:, 7:8, :],
                                br_hi[:, ds(2 * i + b, 1), :].bitcast(F32), ALU.subtract).then_inc(pv_taken, 1)

            def normalized(n, p, dst):
                dve.wait_ge(qk_sqrt, n + 1)
                V.reciprocal(hsum[:], hsum[:]).then_inc(qk_inv, 1)
                dve.wait_ge(qk_inv, n + 1)
                V.tensor_tensor(hscale[:].rearrange("p (t b) -> p t b", b=2), hsum[:].rearrange("p (t b) -> p t b", b=2),
                                rtok[:].unsqueeze(2).broadcast_to([P, TB, 2]), ALU.mult).then_inc(qk_scale, 1)
                dve.wait_ge(qk_scale, n + 1)
                V.tensor_tensor(dst[:].rearrange("p a (g f) -> p (a g) f", f=P),
                                pair(p).rearrange("p a (g f) -> p (a g) f", f=P),
                                hscale[:].unsqueeze(2).broadcast_to([P, 2 * TB, P]), ALU.mult).then_inc(drained[p], 1)

            def gained_lo(o_hi, o_lo, p, r, i, hi_sem, n):
                dve.wait_ge(hi_sem, n + 1)
                for b in range(2):
                    done = V.scalar_tensor_tensor(out=o_lo[:, b:b + 1, :], in0=ps[:, 2 * p + b:2 * p + b + 1, :],
                                                  scalar=par[:, ds(r + 2 * i + b, 1)],
                                                  in1=o_hi[:, b:b + 1, :].bitcast(F32),
                                                  op0=ALU.mult, op1=ALU.subtract)
                done.then_inc(drained[p], 1)

            def attention_pair(l, i, prev):
                T, U = l * T_ALL + T_C + 2 * i, l * U_ALL + U_C + 3 * i
                n = l * NJ + i
                if prev:
                    softmax_head(l, i - 1, 0)
                    softmax_scale(l, i - 1, 0)
                normalized(2 * n, 0, t_a)
                split_lo(0, T + 1)
                if prev:
                    softmax_head(l, i - 1, 1)
                gained_lo(q_hi, q_lo, 0, R_Q, i, q_hi_rdy, n)
                if prev:
                    softmax_scale(l, i - 1, 1)
                normalized(2 * n + 1, 1, t_b)
                split_lo(1, T + 1)
                if prev:
                    probs_lo(l, i - 1, 0)
                gained_lo(k_hi, k_lo, 1, R_K, i, k_hi_rdy, n)
                if prev:
                    heads_lo(l, i - 1, 0)
                    probs_lo(l, i - 1, 1)
                split_lo(0, T + 2)
                if prev:
                    heads_lo(l, i - 1, 1)
                dve.wait_ge(v_hi_rdy, n + 1)
                for t in range(TB):
                    done = V.scalar_tensor_tensor(
                        out=v_lo[:, t, :], in0=ps[:, t // 2, (t % 2) * W:(t % 2 + 1) * W], scalar=rtok[:, t:t + 1],
                        in1=v_hi[:, t, :].bitcast(F32), op0=ALU.mult, op1=ALU.subtract)
                done.then_inc(drained[0], 1)
                take(1, T + 1, U + 2, t_b)
                split_lo(1, T + 2)

            def parameters(l):
                dve.wait_ge(par_mm, l + 2)
                dve.wait_ge(h_rdy, KB * (3 * l + 1))
                V.tensor_copy(par[:, 0:R_Q], ps[:, 7, 0:R_Q])
                V.tensor_scalar(par[:, R_Q:R_Q + KB], ps[:, 7, R_Q:R_Q + KB], SC, None, ALU.mult)
                V.tensor_copy(par[:, R_K:ROWS], ps[:, 7, R_K:ROWS]).then_inc(par_rdy, 1)
                dve.wait_ge(par_rdy, l + 2)
                dve.wait_ge(wf_in, 16 * (l + 1))
                dve.wait_ge(f_mm, FROM + l)
                V.tensor_tensor(wf[:], wf_raw[:], par[:, R_MIX:R_MIX + KB].unsqueeze(2).broadcast_to([P, KB, H]),
                                ALU.mult).then_inc(wf_rdy, 1)

            with dve.Fori(0, L) as l:
                ffn(l, 0, T_UP1, U_UP1, T_DN1, U_DN1, 3 * l, R_MIX, parameters)
                rms_inverse(3 * l + 1)

                dve.wait_ge(f_mm, FROM + l + 1)
                dve.wait_ge(rms_rdy, 3 * l + 2)
                dve.wait_ge(c_out, 16 * FROM + 16 * l)
                V.tensor_tensor(c_neg[:], ps[0:H, 6, :], rinv[0:H, :], ALU.mult).then_inc(f_rows, 1)
                V.memset(z[:, :, 0:2], 0.0).then_inc(z_pad, 1)
                with dve.Fori(0, NJ) as i:
                    T, U, n = l * T_ALL + T_A + 2 * i, l * U_ALL + U_A + 2 * i, l * NJ + i
                    dve.wait_ge(z_pad, l + 1)
                    dve.wait_ge(br_rdy, FROM + 2 * l * NJ + i)
                    take(0, T, U, t_a)
                    split_lo(0, T + 1)
                    dve.wait_ge(gate_rdy, FROM + 3 * l * NJ + i)
                    take(1, T, U, t_b)
                    dve.wait_ge(drained[1], FROM + U + 1)
                    V.tensor_tensor(z[:, :, 2:S + 2], t_a[:], t_b[:], ALU.mult).then_inc(z_rdy, 1)
                    split_lo(1, T + 1)
                    for tap, before, after in ((1, conv0, conv1), (0, conv1, conv2)):
                        dve.wait_ge(before, n + 1)
                        for b in range(2):
                            done = V.scalar_tensor_tensor(
                                out=y_c[:, b:b + 1, :], in0=z[:, b:b + 1, tap:tap + S],
                                scalar=par[:, ds(R_CONV + tap * KB + 2 * i + b, 1)], in1=y_c[:, b:b + 1, :],
                                op0=ALU.mult, op1=ALU.add)
                        done.then_inc(after, 1)
                    dve.wait_ge(tile_done[0], T + 2)
                    V.tensor_tensor(t_a[:], pair(0), over_pair(rinv[:]), ALU.mult).then_inc(drained[0], 1)
                    dve.wait_ge(drained[0], FROM + U + 2)
                    dve.wait_ge(conv2, n + 1)
                    V.tensor_tensor(t_a[:], t_a[:], y_c[:], ALU.mult).then_inc(br_prod, 1)
                    split_lo(0, T + 2)
                    branch_lo(2 * l * NJ + i, i)
                    take(1, T + 1, U + 1, t_b)
                    split_lo(1, T + 2)
                def step(k, ins):
                    ins.then_inc(f_chain, 1)
                    dve.wait_ge(f_chain, 5 * l + k)

                dve.wait_ge(f_turned, l + 1)
                dve.wait_ge(bf_in, 16 * (l + 1))
                step(1, V.tensor_tensor(lf[:, 0], ps[:, 7, 0:TB * H].rearrange("p (t h) -> p t h", h=H),
                                        bf_bc[:].unsqueeze(1).broadcast_to([P, TB, H]), ALU.add))
                V.scalar_tensor_tensor(out=lf[:, 1], in0=lf[:, 0], scalar=-1.0, in1=lf[:, 0],
                                       op0=ALU.mult, op1=ALU.min).then_inc(f_steps, 1)
                dve.wait_ge(f_exp, l + 1)
                V.tensor_scalar(lf[:, 3], lf[:, 2], 1.0, None, ALU.add).then_inc(f_steps, 1)
                dve.wait_ge(f_steps, FROM + 2 * l + 2)
                step(2, V.scalar_tensor_tensor(out=lf[:, 2], in0=lf[:, 3], scalar=-1.0, in1=lf[:, 2],
                                               op0=ALU.add, op1=ALU.subtract))
                step(3, V.reciprocal(lf[:, 5], lf[:, 3]))
                step(4, V.tensor_tensor(lf[:, 2], lf[:, 2], lf[:, 5], ALU.mult))
                dve.wait_ge(f_ln, l + 1)
                step(5, V.scalar_tensor_tensor(out=lf[:, 0], in0=lf[:, 0], scalar=0.0, in1=lf[:, 4],
                                               op0=ALU.min, op1=ALU.subtract))
                V.tensor_tensor(lf[:, 0], lf[:, 0], lf[:, 2], ALU.add).then_inc(f_rdy, 1)
                with dve.Fori(0, 2) as i:
                    for s in range(2):
                        split_lo(s, l * T_ALL + T_BV + i + 1)
                dve.wait_ge(c_mm, l + 1)
                V.tensor_copy(c_tok[:], ps[:, 6, 0:TB * H].rearrange("p (t h) -> p t h", h=H)).then_inc(c_copied, 1)
                V.tensor_scalar(c_neg[:], ps[0:H, 7, :], -1.0, None, ALU.mult).then_inc(c_copied, 1)
                for s in range(2):
                    dve.wait_ge(drained[s], FROM + l * U_ALL + U_WA)
                for t in range(TB):
                    for c in range(2):
                        done = V.bn_stats(stats[:, t, c, :], vn[:, t, c * S:(c + 1) * S])
                done.then_inc(ln_stats, 1)
                dve.wait_ge(ln_stats, l + 1)
                dve.wait_ge(sw_hi_rdy, l + 1)
                V.tensor_tensor(sw_lo[:], ps[:, 4:6, :].rearrange("p a (g t) -> p (a g) t", t=P),
                                sw_hi[:].bitcast(F32), ALU.subtract).then_inc(sw_rdy, 1)
                for t in range(TB):
                    done = V.bn_aggr(mv[:, t, :], stats[:, t, :, :].rearrange("p c k -> p (c k)"))
                done.then_inc(ln_mv, 1)
                dve.wait_ge(ln_sqrt, l + 1)
                V.reciprocal(rstd[:], rstd[:]).then_inc(ln_rstd, 1)
                dve.wait_ge(ln_rstd, l + 1)
                for t in range(TB):
                    V.tensor_scalar(vn[:, t, :], vn[:, t, :], mv[:, t, 0:1], rstd[:, t:t + 1],
                                    ALU.subtract, ALU.mult).then_inc(ln_norm, 1)
                with dve.Fori(0, 2) as i:
                    for s in range(2):
                        dve.wait_ge(gate_rdy, FROM + (3 * l + 1) * NJ)
                        T = l * T_ALL + T_WA + i
                        d = 4 * i + 2 * s
                        dve.wait_ge(tile_done[s], T + 1)
                        V.tensor_tensor(merged[:, ds(d, 2), :], pair(s), gate[:, ds(d, 2), :], ALU.mult).then_inc(drained[s], 1)
                        split_lo(s, T + 1)

                with dve.Fori(0, NJ) as i:
                    T, U, n = l * T_ALL + T_BU + i, l * U_ALL + U_BU + i, l * NJ + i
                    dve.wait_ge(br_rdy, FROM + (2 * l + 1) * NJ + i)
                    dve.wait_ge(vn_rdy, TB * (l + 1))
                    take(0, T, U, t_a)
                    split_lo(0, T + 1)
                    dve.wait_ge(vn_hi_rdy, n + 1)
                    V.tensor_tensor(vn_lo[:], vn[:, :, ds(i * W, W)], vn_hi[:].bitcast(F32), ALU.subtract).then_inc(vns_rdy, 1)
                    dve.wait_ge(gate_rdy, FROM + (3 * l + 1) * NJ + i)
                    take(1, T, U, t_b)
                    split_lo(1, T + 1)
                    dve.wait_ge(sp_mm, FROM + n + 1)
                    for b in range(2):
                        done = V.tensor_tensor(
                            y_c[:, b, :].rearrange("p (t s) -> p t s", s=P), ps[:, 4 + b, :].rearrange("p (t s) -> p t s", s=P),
                            bs_bc[:, ds(2 * i + b, 1), :].broadcast_to([P, TB, P]), ALU.add)
                    done.then_inc(sp_added, 1)
                    dve.wait_ge(sp_added, FROM + n + 1)
                    dve.wait_ge(gelu_rdy, n + 1)
                    V.tensor_tensor(t_a[:], t_a[:], y_c[:], ALU.mult).then_inc(br_prod, 1)
                    branch_lo((2 * l + 1) * NJ + i, i)
                with dve.Fori(0, 2) as i:
                    for s in range(2):
                        dve.wait_ge(gate_rdy, FROM + (3 * l + 2) * NJ)
                        T, U, t = l * T_ALL + T_WB + i, l * U_ALL + U_WB + i, (t_a, t_b)[s]
                        dve.wait_ge(br_rdy, FROM + (2 * l + 2) * NJ)
                        dve.wait_ge(mg_add, FROM + 8 * l + 2 * i)
                        d = 4 * i + 2 * s
                        dve.wait_ge(tile_done[s], T + 1)
                        V.tensor_tensor(t[:], pair(s), gate[:, ds(d, 2), :], ALU.mult).then_inc(drained[s], 1)
                        dve.wait_ge(drained[s], FROM + U + 1)
                        V.tensor_tensor(merged[:, ds(d, 2), :], merged[:, ds(d, 2), :], t[:], ALU.add).then_inc(mg_add, 1)
                        split_lo(s, T + 1)
                attention_pair(l, 0, False)
                with dve.Fori(1, NJ) as i:
                    attention_pair(l, i, True)
                softmax_head(l, NJ - 1, 0)
                softmax_head(l, NJ - 1, 1)
                softmax_scale(l, NJ - 1, 0)
                probs_lo(l, NJ - 1, 0)
                softmax_scale(l, NJ - 1, 1)
                heads_lo(l, NJ - 1, 0)
                probs_lo(l, NJ - 1, 1)
                heads_lo(l, NJ - 1, 1)
                with dve.Fori(0, 2) as i:
                    for s in range(2):
                        dve.wait_ge(gate_rdy, FROM + (3 * l + 3) * NJ)
                        T, U, t = l * T_ALL + T_WC + i, l * U_ALL + U_WC + i, (t_a, t_b)[s]
                        d, n = 4 * i + 2 * s, 4 * l + 2 * i + s
                        dve.wait_ge(m_rdy, FROM + 4 * l + 2 * i)
                        dve.wait_ge(tile_done[s], T + 1)
                        V.tensor_tensor(t[:], pair(s), gate[:, ds(d, 2), :], ALU.mult).then_inc(drained[s], 1)
                        dve.wait_ge(drained[s], FROM + U + 1)
                        V.tensor_tensor(t[:], merged[:, ds(d, 2), :], t[:], ALU.add).then_inc(mg_add, 1)
                        split_lo(s, T + 1)
                        dve.wait_ge(m_hi_rdy, n + 1)
                        V.tensor_tensor(m_lo[:, ds(d, 2), :], t[:], m_hi[:, ds(d, 2), :].bitcast(F32),
                                        ALU.subtract).then_inc(m_rdy, 1)
                with dve.Fori(0, 2) as i:
                    for s in range(2):
                        T, U, d = l * T_ALL + T_WO + i, l * U_ALL + U_WO + i, 4 * i + 2 * s
                        dve.wait_ge(tile_done[s], T + 1)
                        V.tensor_tensor(xT[:, ds(d, 2), :], pair(s), xT[:, ds(d, 2), :], ALU.add).then_inc(drained[s], 1)
                        dve.wait_ge(drained[s], FROM + U + 1)
                        h_blocks(d, 2, R_FFN2, KB * (3 * l + 2) + d + 2)
                        split_lo(s, T + 1)
                ffn(l, 1, T_UP2, U_UP2, T_DN2, U_DN2, 3 * l + 2, R_NEXT)
            for t in (0, 2):
                dve.wait_ge(y_mm, t + 1)
                if t:
                    dve.wait_ge(y_copied, t)
                V.tensor_copy(x_io[:, t, :], ps[:, 2 * t:2 * t + 2, :].rearrange("p a s -> p (a s)")).then_inc(y_copied, 1)

        @block.gpsimd
        def _(pool):
            G = nc.gpsimd

            def causal(m, op, fill, step, chan):
                G.affine_select(out=m[:], in_=m[:], compare_op=op, fill=fill, base=0,
                                pattern=[[step, P]], channel_multiplier=chan).then_inc(const_rdy, 1)

            G.memset(eps_rms[:], RMS_EPS)
            G.memset(eps_ln[:], LN_EPS)
            G.memset(ones[:], 1.0)
            G.memset(ident[:], 0.0)
            G.memset(ident_b[:], 0.0)
            G.memset(causal_b[:], 0.0)
            G.memset(lower[:], 1.0)
            G.memset(upper[:], 1.0).then_inc(const_rdy, 1)
            pool.wait_ge(const_rdy, 1)
            causal(ident, ALU.not_equal, 1.0, -1, 1)
            causal(ident_b, ALU.not_equal, 1.0, -1, 1)
            causal(causal_b, ALU.is_ge, MASKED, -1, 1)
            causal(upper, ALU.is_ge, 0.0, 1, -1)
            causal(lower, ALU.is_ge, 0.0, -1, 1)

            def first_square(n):
                if not (isinstance(n, int) and n == 0):
                    pool.wait_ge(rms_mm, n)
                G.tensor_tensor(sq[:, 1, :], xT[:, 0, :], xT[:, 0, :], ALU.mult).then_inc(ssq_rdy, 1)

            def squares(n, d):
                pool.wait_ge(ssq_rdy, KB * n + d)
                G.tensor_tensor(sq[:, 0:1, :], xT[:, ds(d, 1), :], xT[:, ds(d, 1), :], ALU.mult).then_inc(sq_rdy, 1)
                pool.wait_ge(sq_rdy, (KB - 1) * n + d)
                G.tensor_tensor(sq[:, 1:2, :], sq[:, 1:2, :], sq[:, 0:1, :], ALU.add).then_inc(ssq_rdy, 1)

            pool.wait_ge(x_copied, 1)
            first_square(0)
            with pool.Fori(1, KB) as d:
                pool.wait_ge(x_copied, d + 1)
                squares(0, d)

            def ffn(l, u_dn, norm):
                pool.wait_ge(drained[0], FROM + l * U_ALL + u_dn + 1)
                first_square(norm)
                pool.wait_ge(drained[1], FROM + l * U_ALL + u_dn + 1)
                squares(norm, 1)
                with pool.Fori(1, KB // 2) as i:
                    for e in range(2):
                        pool.wait_ge(drained[e], FROM + l * U_ALL + u_dn + i + 1)
                        squares(norm, 2 * i + e)

            with pool.Fori(0, L) as l:
                ffn(l, U_DN1, 3 * l + 1)
                pool.wait_ge(sw_in, 16 * (l + 1))
                pool.wait_ge(const_rdy, CONSTS)
                G.tensor_tensor(sw_raw[:], sw_raw[:], lower[:].unsqueeze(1).broadcast_to([P, H, P]),
                                ALU.mult).then_inc(sw_masked, 1)
                pool.wait_ge(lng_in, 16 * (l + 1))
                pool.wait_ge(lnb_in, 16 * (l + 1))
                for t in range(TB):
                    pool.wait_ge(ln_norm, TB * l + t + 1)
                    G.tensor_tensor(vn[:, t, :], vn[:, t, :], ln_g, ALU.mult).then_inc(ln_gained, 1)
                    pool.wait_ge(ln_gained, TB * l + t + 1)
                    G.tensor_tensor(vn[:, t, :], vn[:, t, :], ln_b, ALU.add).then_inc(vn_rdy, 1)
                pool.wait_ge(s_taken, FROM + (l + 1) * H)
                pool.wait_ge(drained[0], FROM + l * U_ALL + U_WO + 1)
                first_square(3 * l + 2)
                squares(3 * l + 2, 1)
                pool.wait_ge(drained[1], FROM + l * U_ALL + U_WO + 1)
                squares(3 * l + 2, 2)
                squares(3 * l + 2, 3)
                with pool.Fori(1, 2) as i:
                    for s in range(2):
                        pool.wait_ge(drained[s], FROM + l * U_ALL + U_WO + i + 1)
                        for b in range(2):
                            squares(3 * l + 2, 4 * i + 2 * s + b)
                ffn(l, U_DN2, 3 * l + 3)


_INS = ["x", "ffn1_norm", "ffn1_w_gu", "ffn1_w_down", "mix_norm", "w_in", "b_forget", "b_gate", "conv_w",
        "sgu_ln_g", "sgu_ln_b", "sgu_w", "sgu_b", "q_norm_g", "k_norm_g", "w_out_conv", "w_out_sgu",
        "w_out_attn", "w_o", "ffn2_norm", "ffn2_w_gu", "ffn2_w_down"]


def kernel(**inputs):
    import numpy as _np
    import concourse.bacc as _bacc
    from concourse.bass_utils import run_bass_kernel_spmd as _run

    nc = _bacc.Bacc("TRN2", target_bir_lowering=False, num_devices=1, dynamic_dma_scratch_size=1024)
    arrays, args = {}, []
    for name in _INS:
        a = _np.ascontiguousarray(inputs[name])
        arrays[f"in_{name}_dram"] = a
        args.append(nc.dram_tensor(f"in_{name}_dram", a.shape, mybir.dt.from_np(a.dtype), kind="ExternalInput").ap())
    out = nc.dram_tensor("out_0_dram", inputs["x"].shape, F32, kind="ExternalOutput").ap()
    build(nc, *args, out)
    r = _run(nc, [arrays], core_ids=[0])
    return r.results[0]["out_0_dram"]
```
